# Optimizing a Trainium2 kernel written in Bass

```python
import math
import jax, jax.numpy as jnp
from jax import lax
import numpy as np

D_MODEL = 1024
BATCH = 1
SEQ = 256
DEPTH = 2

HEAD_DIM = 64
S5_WIDTH = D_MODEL // 4
S5_GROUP = 16
S5_GROUPS = S5_WIDTH // S5_GROUP
S5_STATE = 64
MOBA_WIDTH = 3 * D_MODEL // 8
MOBA_HEADS = MOBA_WIDTH // HEAD_DIM
GDN_WIDTH = 3 * D_MODEL // 8
GDN_HEADS = GDN_WIDTH // HEAD_DIM
MIX_WIDTH = S5_WIDTH + MOBA_WIDTH + GDN_WIDTH
IN_SIZES = (S5_WIDTH, MOBA_WIDTH, MOBA_WIDTH, MOBA_WIDTH,
            GDN_WIDTH, GDN_WIDTH, GDN_WIDTH, GDN_WIDTH, GDN_HEADS, GDN_HEADS)
IN_COLS = sum(IN_SIZES)

MOBA_BLOCK = 256
MOBA_TOPK = 3
MOBA_QBLOCK = 32
GDN_CHUNK = 64
CONV_WIDTH = 4

D_FF = 7 * D_MODEL // 2
N_EXPERTS = 8
TOP_K = 2
N_DENSE = (DEPTH + 1) // 2
N_MOE = DEPTH // 2

DEEPNORM_ALPHA = (2 * DEPTH) ** 0.25
DEEPNORM_BETA = (8 * DEPTH) ** -0.25
LN_EPS = 1e-5
RMS_EPS = 1e-6

kernel_name = "hymba_s5_moba_gdn_deepnorm_moe"

F32 = jnp.float32

def _split(h, sizes):
    idx = np.cumsum(np.array(sizes))[:-1].tolist()
    return jnp.split(h, idx, axis=-1)

def layer_norm(x, g, b):
    xf = x.astype(F32)
    mu = jnp.mean(xf, axis=-1, keepdims=True)
    var = jnp.mean(jnp.square(xf - mu), axis=-1, keepdims=True)
    return ((xf - mu) * lax.rsqrt(var + LN_EPS) * g.astype(F32) + b.astype(F32)).astype(x.dtype)

def l2norm(t):
    return t * lax.rsqrt(jnp.sum(jnp.square(t), axis=-1, keepdims=True) + RMS_EPS)

def s5_mixer(u, lam_re, lam_im, log_dt, b_re, b_im, c_re, c_im, d_skip, glu_w, glu_b):
    bsz, seqlen, _ = u.shape
    lam = lax.complex(lam_re.astype(F32), lam_im.astype(F32))
    step = jnp.exp(log_dt.astype(F32))[:, None]
    lam_bar = jnp.exp(lam * step)
    b_mat = lax.complex(b_re.astype(F32), b_im.astype(F32))
    b_bar = ((lam_bar - 1.0) / lam)[..., None] * b_mat
    ug = u.astype(F32).reshape(bsz, seqlen, S5_GROUPS, S5_GROUP)
    bu = jnp.einsum('blgp,gnp->blgn', ug.astype(jnp.complex64), b_bar)
    a = jnp.broadcast_to(lam_bar, bu.shape)

    def combine(e1, e2):
        a1, s1 = e1
        a2, s2 = e2
        return a1 * a2, a2 * s1 + s2

    _, states = lax.associative_scan(combine, (a, bu), axis=1)
    c_mat = lax.complex(c_re.astype(F32), c_im.astype(F32))
    y = jnp.einsum('gpn,blgn->blgp', c_mat, states).real + d_skip.astype(F32) * ug
    y = jax.nn.gelu(y.reshape(bsz, seqlen, S5_WIDTH))
    y = y * jax.nn.sigmoid(y @ glu_w.astype(F32) + glu_b.astype(F32))
    return y.astype(u.dtype)

def moba_mixer(q, k, v):
    bsz, seqlen, _ = q.shape
    n_blocks = -(-seqlen // MOBA_BLOCK)
    lpad = n_blocks * MOBA_BLOCK

    def heads(t):
        t = t.reshape(bsz, seqlen, MOBA_HEADS, HEAD_DIM).transpose(0, 2, 1, 3).astype(F32)
        return jnp.pad(t, ((0, 0), (0, 0), (0, lpad - seqlen), (0, 0)))

    qh = heads(q) * HEAD_DIM ** -0.5
    kh, vh = heads(k), heads(v)
    kb = kh.reshape(bsz, MOBA_HEADS, n_blocks, MOBA_BLOCK, HEAD_DIM)
    vb = vh.reshape(bsz, MOBA_HEADS, n_blocks, MOBA_BLOCK, HEAD_DIM)
    kmean = jnp.mean(kb, axis=3)

    gate = jnp.einsum('bhld,bhnd->bhln', qh, kmean)
    qblk = jnp.arange(lpad) // MOBA_BLOCK
    past = jnp.arange(n_blocks)[None, :] < qblk[:, None]
    gate = jnp.where(past, gate, -jnp.inf)
    n_sel = min(MOBA_TOPK, n_blocks)
    sel_score, sel_idx = lax.top_k(gate, n_sel)
    sel_valid = jnp.isfinite(sel_score)

    n_qb = lpad // MOBA_QBLOCK

    def by_qblock(t):
        t = t.reshape(bsz, MOBA_HEADS, n_qb, MOBA_QBLOCK, *t.shape[3:])
        return jnp.moveaxis(t, 2, 0)

    b_ix = jnp.arange(bsz)[:, None, None, None]
    h_ix = jnp.arange(MOBA_HEADS)[None, :, None, None]

    def attend(args):
        qc, idx, valid, i = args
        qpos = i * MOBA_QBLOCK + jnp.arange(MOBA_QBLOCK)
        own = (i * MOBA_QBLOCK) // MOBA_BLOCK
        k_own = lax.dynamic_index_in_dim(kb, own, axis=2, keepdims=False)
        v_own = lax.dynamic_index_in_dim(vb, own, axis=2, keepdims=False)
        kpos = own * MOBA_BLOCK + jnp.arange(MOBA_BLOCK)
        s_own = jnp.einsum('bhqd,bhkd->bhqk', qc, k_own)
        s_own = jnp.where(kpos[None, :] <= qpos[:, None], s_own, -jnp.inf)
        k_sel = kb[b_ix, h_ix, idx]
        v_sel = vb[b_ix, h_ix, idx]
        s_sel = jnp.einsum('bhqd,bhqnkd->bhqnk', qc, k_sel)
        s_sel = jnp.where(valid[..., None], s_sel, -jnp.inf)
        s_sel = s_sel.reshape(*s_sel.shape[:3], n_sel * MOBA_BLOCK)
        p = jax.nn.softmax(jnp.concatenate([s_own, s_sel], axis=-1), axis=-1)
        p_own = p[..., :MOBA_BLOCK]
        p_sel = p[..., MOBA_BLOCK:].reshape(*p.shape[:3], n_sel, MOBA_BLOCK)
        return (jnp.einsum('bhqk,bhkd->bhqd', p_own, v_own)
                + jnp.einsum('bhqnk,bhqnkd->bhqd', p_sel, v_sel))

    o = lax.map(attend, (by_qblock(qh), by_qblock(sel_idx), by_qblock(sel_valid), jnp.arange(n_qb)))
    o = jnp.moveaxis(o, 0, 2).reshape(bsz, MOBA_HEADS, lpad, HEAD_DIM)[:, :, :seqlen]
    return o.transpose(0, 2, 1, 3).reshape(bsz, seqlen, MOBA_WIDTH).astype(q.dtype)

def causal_conv(x, w):
    ch = x.shape[-1]
    return lax.conv_general_dilated(x, w[:, None, :].astype(x.dtype), window_strides=(1,),
                                    padding=[(CONV_WIDTH - 1, 0)],
                                    dimension_numbers=('NWC', 'WIO', 'NWC'),
                                    feature_group_count=ch)

def chunk_gated_delta(q, k, v, g, beta):
    bsz, nh, seqlen, dk = q.shape
    dv = v.shape[-1]
    n = seqlen // GDN_CHUNK
    C = GDN_CHUNK
    q = q.reshape(bsz, nh, n, C, dk)
    k = k.reshape(bsz, nh, n, C, dk)
    v = v.reshape(bsz, nh, n, C, dv)
    g = jnp.cumsum(g.reshape(bsz, nh, n, C), axis=-1)
    beta = beta.reshape(bsz, nh, n, C)
    kb = k * beta[..., None]
    vb = v * beta[..., None]
    tril_incl = jnp.tril(jnp.ones((C, C), dtype=bool))
    tril_strict = jnp.tril(jnp.ones((C, C), dtype=bool), -1)
    diff = jnp.where(tril_incl, g[..., :, None] - g[..., None, :], 0.0)
    decay = jnp.where(tril_incl, jnp.exp(diff), 0.0)
    lmat = jnp.where(tril_strict, jnp.einsum('bhncd,bhnsd->bhncs', kb, k) * decay, 0.0)
    eye = jnp.eye(C, dtype=F32)
    rhs = jnp.concatenate([vb, kb * jnp.exp(g)[..., None]], axis=-1)
    sol = lax.linalg.triangular_solve(eye + lmat, rhs, left_side=True, lower=True,
                                      unit_diagonal=True)
    u_val, w_k = sol[..., :dv], sol[..., dv:]
    attn = jnp.where(tril_incl, jnp.einsum('bhncd,bhnsd->bhncs', q, k) * decay, 0.0)

    def step(S, inp):
        qc, kc, uc, wc, gc, ac = inp
        v_new = uc - jnp.einsum('bhcd,bhde->bhce', wc, S)
        o = (jnp.einsum('bhcd,bhde->bhce', qc * jnp.exp(gc)[..., None], S)
             + jnp.einsum('bhcs,bhse->bhce', ac, v_new))
        g_last = gc[..., -1:]
        S = (S * jnp.exp(g_last)[..., None]
             + jnp.einsum('bhcd,bhce->bhde', kc * jnp.exp(g_last - gc)[..., None], v_new))
        return S, o

    xs = tuple(jnp.moveaxis(t, 2, 0) for t in (q, k, u_val, w_k, g, attn))
    S0 = jnp.zeros((bsz, nh, dk, dv), F32)
    _, o = lax.scan(step, S0, xs)
    return jnp.moveaxis(o, 0, 2).reshape(bsz, nh, seqlen, dv)

def gdn_mixer(q, k, v, z, a, b, conv_w, a_log, dt_bias, norm_w):
    bsz, seqlen, _ = q.shape
    qkv = jax.nn.silu(causal_conv(jnp.concatenate([q, k, v], axis=-1), conv_w).astype(F32))
    q, k, v = _split(qkv, (GDN_WIDTH, GDN_WIDTH, GDN_WIDTH))

    def heads(t):
        return t.reshape(bsz, seqlen, GDN_HEADS, HEAD_DIM).transpose(0, 2, 1, 3)

    qh = l2norm(heads(q)) * HEAD_DIM ** -0.5
    kh = l2norm(heads(k))
    vh = heads(v)
    beta = jax.nn.sigmoid(b.astype(F32)).transpose(0, 2, 1)
    g = (-jnp.exp(a_log.astype(F32))
         * jax.nn.softplus(a.astype(F32) + dt_bias.astype(F32))).transpose(0, 2, 1)
    o = chunk_gated_delta(qh, kh, vh, g, beta).transpose(0, 2, 1, 3)
    zh = z.astype(F32).reshape(bsz, seqlen, GDN_HEADS, HEAD_DIM)
    o = (o * lax.rsqrt(jnp.mean(jnp.square(o), axis=-1, keepdims=True) + RMS_EPS)
         * norm_w.astype(F32) * jax.nn.silu(zh))
    return o.reshape(bsz, seqlen, GDN_WIDTH).astype(q.dtype)

def swiglu(x, w_gate, w_up, w_down):
    return (jax.nn.silu(x @ w_gate) * (x @ w_up)) @ w_down

def moe_ffn(x, router_w, w_gate, w_up, w_down):
    logits = (x @ router_w).astype(F32)
    top_val, top_idx = lax.top_k(logits, TOP_K)
    gates = jax.nn.softmax(top_val, axis=-1)
    combine = jnp.sum(jax.nn.one_hot(top_idx, N_EXPERTS, dtype=F32) * gates[..., None], axis=-2)
    out = jnp.zeros(x.shape, F32)
    for e in range(N_EXPERTS):
        out = out + combine[..., e:e + 1] * swiglu(x, w_gate[e], w_up[e], w_down[e]).astype(F32)
    return out.astype(x.dtype)

def setup_inputs(seed: int = 0) -> dict:
    key = jax.random.key(seed)
    ks = jax.random.split(key, 32)
    nrm = jax.random.normal
    G, N, P = S5_GROUPS, S5_STATE, S5_GROUP
    x = nrm(ks[0], (BATCH, SEQ, D_MODEL), F32)
    w_in = nrm(ks[1], (DEPTH, D_MODEL, IN_COLS), F32) * D_MODEL ** -0.5
    w_out = nrm(ks[2], (DEPTH, MIX_WIDTH, D_MODEL), F32) * MIX_WIDTH ** -0.5 * DEEPNORM_BETA
    s5_lam_re = -0.5 + 0.01 * nrm(ks[3], (DEPTH, G, N), F32)
    s5_lam_im = (jnp.pi * jnp.arange(N, dtype=F32))[None, None, :] + 0.01 * nrm(ks[4], (DEPTH, G, N), F32)
    s5_log_dt = jax.random.uniform(ks[5], (DEPTH, G), F32, math.log(1e-3), math.log(1e-1))
    s5_b_re = nrm(ks[6], (DEPTH, G, N, P), F32) * (2 * P) ** -0.5
    s5_b_im = nrm(ks[7], (DEPTH, G, N, P), F32) * (2 * P) ** -0.5
    s5_c_re = nrm(ks[8], (DEPTH, G, P, N), F32) * (2 * N) ** -0.5
    s5_c_im = nrm(ks[9], (DEPTH, G, P, N), F32) * (2 * N) ** -0.5
    s5_d = nrm(ks[10], (DEPTH, G, P), F32)
    s5_glu_w = nrm(ks[11], (DEPTH, S5_WIDTH, S5_WIDTH), F32) * S5_WIDTH ** -0.5
    s5_glu_b = 0.01 * nrm(ks[12], (DEPTH, S5_WIDTH), F32)
    gdn_conv_w = nrm(ks[13], (DEPTH, CONV_WIDTH, 3 * GDN_WIDTH), F32) * CONV_WIDTH ** -0.5
    gdn_a_log = jnp.log(jax.random.uniform(ks[14], (DEPTH, GDN_HEADS), F32, 1.0, 16.0))
    dt0 = jnp.exp(jax.random.uniform(ks[15], (DEPTH, GDN_HEADS), F32, math.log(1e-3), math.log(1e-1)))
    gdn_dt_bias = dt0 + jnp.log(-jnp.expm1(-dt0))
    gdn_norm_w = 1.0 + 0.01 * nrm(ks[16], (DEPTH, HEAD_DIM), F32)
    ln1_g = 1.0 + 0.01 * nrm(ks[17], (DEPTH, D_MODEL), F32)
    ln1_b = 0.01 * nrm(ks[18], (DEPTH, D_MODEL), F32)
    ln2_g = 1.0 + 0.01 * nrm(ks[19], (DEPTH, D_MODEL), F32)
    ln2_b = 0.01 * nrm(ks[20], (DEPTH, D_MODEL), F32)
    ffn_w_gate = nrm(ks[21], (N_DENSE, D_MODEL, D_FF), F32) * D_MODEL ** -0.5
    ffn_w_up = nrm(ks[22], (N_DENSE, D_MODEL, D_FF), F32) * D_MODEL ** -0.5
    ffn_w_down = nrm(ks[23], (N_DENSE, D_FF, D_MODEL), F32) * D_FF ** -0.5 * DEEPNORM_BETA
    moe_router = nrm(ks[24], (N_MOE, D_MODEL, N_EXPERTS), F32) * D_MODEL ** -0.5
    moe_w_gate = nrm(ks[25], (N_MOE, N_EXPERTS, D_MODEL, D_FF), F32) * D_MODEL ** -0.5
    moe_w_up = nrm(ks[26], (N_MOE, N_EXPERTS, D_MODEL, D_FF), F32) * D_MODEL ** -0.5
    moe_w_down = nrm(ks[27], (N_MOE, N_EXPERTS, D_FF, D_MODEL), F32) * D_FF ** -0.5 * DEEPNORM_BETA
    return {"x": x, "w_in": w_in, "w_out": w_out,
            "s5_lam_re": s5_lam_re, "s5_lam_im": s5_lam_im, "s5_log_dt": s5_log_dt,
            "s5_b_re": s5_b_re, "s5_b_im": s5_b_im, "s5_c_re": s5_c_re, "s5_c_im": s5_c_im,
            "s5_d": s5_d, "s5_glu_w": s5_glu_w, "s5_glu_b": s5_glu_b,
            "gdn_conv_w": gdn_conv_w, "gdn_a_log": gdn_a_log, "gdn_dt_bias": gdn_dt_bias,
            "gdn_norm_w": gdn_norm_w,
            "ln1_g": ln1_g, "ln1_b": ln1_b, "ln2_g": ln2_g, "ln2_b": ln2_b,
            "ffn_w_gate": ffn_w_gate, "ffn_w_up": ffn_w_up, "ffn_w_down": ffn_w_down,
            "moe_router": moe_router, "moe_w_gate": moe_w_gate, "moe_w_up": moe_w_up,
            "moe_w_down": moe_w_down}

def reference(x, w_in, w_out, s5_lam_re, s5_lam_im, s5_log_dt, s5_b_re, s5_b_im, s5_c_re,
              s5_c_im, s5_d, s5_glu_w, s5_glu_b, gdn_conv_w, gdn_a_log, gdn_dt_bias, gdn_norm_w,
              ln1_g, ln1_b, ln2_g, ln2_b, ffn_w_gate, ffn_w_up, ffn_w_down,
              moe_router, moe_w_gate, moe_w_up, moe_w_down):
    for l in range(DEPTH):
        h = x @ w_in[l]
        s5_u, mq, mk, mv, gq, gk, gv, gz, ga, gb = _split(h, IN_SIZES)
        y_s5 = s5_mixer(s5_u, s5_lam_re[l], s5_lam_im[l], s5_log_dt[l], s5_b_re[l], s5_b_im[l],
                        s5_c_re[l], s5_c_im[l], s5_d[l], s5_glu_w[l], s5_glu_b[l])
        y_moba = moba_mixer(mq, mk, mv)
        y_gdn = gdn_mixer(gq, gk, gv, gz, ga, gb, gdn_conv_w[l], gdn_a_log[l], gdn_dt_bias[l],
                          gdn_norm_w[l])
        mix = jnp.concatenate([y_s5, y_moba, y_gdn], axis=-1) @ w_out[l]
        x = layer_norm(DEEPNORM_ALPHA * x + mix, ln1_g[l], ln1_b[l])
        if l % 2 == 0:
            f = swiglu(x, ffn_w_gate[l // 2], ffn_w_up[l // 2], ffn_w_down[l // 2])
        else:
            f = moe_ffn(x, moe_router[l // 2], moe_w_gate[l // 2], moe_w_up[l // 2], moe_w_down[l // 2])
        x = layer_norm(DEEPNORM_ALPHA * x + f, ln2_g[l], ln2_b[l])
    return x


_drawn_inputs = setup_inputs


def setup_inputs(seed=0):
    import zlib

    import numpy as np

    out = dict(_drawn_inputs(seed))
    spreads = {}
    factors = {'s5_lam_re': 64.0,
     's5_lam_im': 44.224,
     's5_log_dt': 59.808,
     's5_b_re': 64.0,
     's5_b_im': 45.48,
     's5_c_re': 64.0,
     's5_c_im': 62.664,
     's5_glu_b': 64.0,
     'gdn_norm_w': 8.0,
     'ln1_g': 2.857,
     'ln1_b': 2.983,
     'ln2_g': 2.695,
     'ln2_b': 3.216}
    for name, (base, spread) in spreads.items():
        noise = np.random.default_rng([zlib.crc32(name.encode()), seed]).standard_normal(out[name].shape)
        drawn = base * np.exp(spread * noise) if base else spread * noise
        out[name] = __import__('jax').numpy.asarray(drawn.astype(out[name].dtype))
    for name, factor in factors.items():
        out[name] = (out[name] * factor).astype(out[name].dtype)
    return out
```

```python
from contextlib import ExitStack

import numpy as np
import concourse.bass as bass
from concourse import mybir

ALU = mybir.AluOpType
ACT = mybir.ActivationFunctionType
F32 = mybir.dt.float32
I32 = mybir.dt.int32
AX_X = mybir.AxisListType.X

P = 128
D = 1024
T = 256
L = 2
NB = T // P
KT = D // P
S5W, MBW, GDW = 256, 384, 384
HD = 64
NH = 6
CH = 64
NC = T // CH
ST = 8
FF = 3584
FC = FF // 512
NE = 8
ALPHA = float((2 * L) ** 0.25)
SCALE = HD ** -0.5
NEG = -1.0e30

C_U, C_Q, C_K, C_V = 0, 256, 640, 1024
C_G, C_Z = 1408, 2560
IN_COLS = 2956
ZAB = IN_COLS - C_Z
WIN = [(0, 512), (512, 512), (1024, 384), (1408, 512), (1920, 512), (2432, 524)]
SLOT = KT * 524
SLOTS = 4
NSLOT = 7
PER_LAYER = len(WIN) + 2
N_DENSE = 3 * FC
FIRST = [0, PER_LAYER + N_DENSE]
N_PRE = 2 * PER_LAYER + N_DENSE
EXP = 3 * FC
assert EXP % NSLOT == 0

_names = ["ident", "cum", "same", "ch0", "ch1", "ones", "causal", "negu", "lv0", "lv1", "lv2", "lv3", "lv4", "lv5",
          "before", "iota"]
CO = {n: 128 * i for i, n in enumerate(_names)}
C_REV = 128 * len(_names)
C_EPS6, C_EPS5, C_HPI, C_ONE = C_REV + 8, C_REV + 9, C_REV + 10, C_REV + 11
CW = C_REV + 12


def constant_table():
    r = np.arange(P)
    a, b = r[:, None], r[None, :]
    same = (a // CH) == (b // CH)
    c = np.zeros((P, CW), np.float32)

    def put(name, v):
        c[:, CO[name]:CO[name] + P] = v

    put("ident", a == b)
    put("cum", (a <= b) & same)
    put("same", same)
    put("ch0", a < CH)
    put("ch1", a >= CH)
    put("ones", 1.0)
    put("causal", np.where(b <= a, 0.0, NEG))
    put("negu", np.where((a <= b) & same, 0.0, NEG))
    for v in range(6):
        s = 1 << v
        put(f"lv{v}", ((b // s) % 2 == 1) & (a // s == b // s - 1))
    put("before", a < b)
    put("iota", np.broadcast_to(b, (P, P)))
    c[:, C_REV:C_REV + NE] = NE - np.arange(NE)
    c[:, C_EPS6], c[:, C_EPS5], c[:, C_HPI], c[:, C_ONE] = 1e-6, 1e-5, np.pi / 2, 1.0
    return c


PO, PW = {}, 0
for _n, _w in (("lre", L * ST), ("lim", L * ST), ("ldt", L * ST), ("d", L * 2), ("gb", L * 2), ("conv", L * 36),
               ("alog", L * NH), ("dtb", L * NH), ("nw", L * HD), ("c", L * ST * 32), ("router", KT * NE)):
    PO[_n] = PW
    PW += _w

ZS = (NSLOT - SLOTS) * SLOT
ZF = 9248
O_BP, O_CP, O_M, O_S = 0, 2304, 4352, 8448
O_PT = 0
O_DT, O_U, O_T, O_A, O_MM, O_LA = 0, 1536, 3072, 4608, 6144, 9216
O_SQ, O_RN, O_TG = 4608, 6144, 7680
O_SIG = 12032
O_QKV, O_Z = 0, 2304
O_UT, O_QKM, O_MV, O_CIN, O_Y, O_GW = 3072, 3584, 5120, 5888, 8224, 8736
O_KV, O_KG, O_KD, O_UP, O_WT, O_VP, O_O, O_ST = 3072, 4608, 5376, 6144, 6912, 7680, 8448, 3072
O_SG, O_H, O_HT, O_XG, O_P, O_PW, O_PWT, O_YE, O_FA = 0, 1024, 2048, 3072, 4096, 4352, 4608, 4864, 5888


def build(nc, x_in, w_in, w_out, consts, params, s5_b, glu_w, ln, wg, wu, wd, mg, mu, md, out):
    ctx = ExitStack()
    with ctx:
        def sb(name, cols, dt=F32):
            return ctx.enter_context(nc.sbuf_tensor(name, [P, cols], dt))

        sems = {}

        def sem(name):
            sems[name] = ctx.enter_context(nc.semaphore(name))
            return sems[name]

        ring = sb("ring", SLOTS * SLOT)
        zone_s = sb("zone_s", ZS)
        zone_f = sb("zone_f", ZF)
        x = sb("x", NB * D)[:, :].rearrange("p (b d) -> p b d", b=NB)
        xT = sb("xT", KT * T)[:, :].rearrange("p (k t) -> p k t", k=KT)
        cst = sb("cst", CW)
        par = sb("par", PW)
        score_rows = sb("score_rows", NH * 3 * P)
        lnrow = score_rows[:, 0:2 * D].rearrange("p (g d) -> p g d", g=2)
        phase = sb("phase", 2 * ST * T)
        s5s = sb("s5s", 24 * L * ST)
        small = sb("small", 256)
        count_i = sb("count_i", 2, I32)
        pos = sb("pos", 2 * 17)[:, :].rearrange("p (b e) -> p b e", b=2)
        comb = sb("comb", 2 * 17)[:, :].rearrange("p (b e) -> p b e", b=2)
        rt = sb("rt", 160)
        ps = ctx.enter_context(nc.psum_tensor("ps", [P, 8, 512], F32))

        def C(name, rows=slice(0, P)):
            return cst[rows, CO[name]:CO[name] + P]

        ident = C("ident")

        def slot(s):
            return ring[:, s * SLOT:(s + 1) * SLOT] if s < SLOTS else \
                zone_s[:, (s - SLOTS) * SLOT:(s - SLOTS + 1) * SLOT]

        def zs(o, n):
            return zone_s[:, o:o + n]

        def zf(o, n):
            return zone_f[:, o:o + n]

        cos_t = phase[:, 0:ST * T].rearrange("p (j t) -> p j t", j=ST)
        sin_t = phase[:, ST * T:2 * ST * T].rearrange("p (j t) -> p j t", j=ST)
        b_pad = zs(O_BP, 2048).rearrange("p (j r s) -> p j r s", j=ST, r=2)
        c_pad = zs(O_CP, 2048).rearrange("p (j r f) -> p j r f", j=ST, r=2)
        mt = [zs(O_M + 1024 * i, 1024) for i in range(4)]
        states = [zs(O_S + 2048 * r, 2048).rearrange("p (j t) -> p j t", j=ST) for r in range(2)]
        uT = zf(O_UT, 512).rearrange("p (f t) -> p f t", f=2)
        gw = zf(O_GW, 512).rearrange("p (k n) -> p k n", k=2)
        ys = zf(O_Y, 512).rearrange("p (f t) -> p f t", f=2)
        sig = zs(O_SIG, 512).rearrange("p (f t) -> p f t", f=2)
        qkm = zf(O_QKM, 1536).rearrange("p (t n) -> p t n", t=6)
        mv = zf(O_MV, 768).rearrange("p (b n) -> p b n", b=2)
        sc = score_rows[:, :].rearrange("p (h n) -> p h n", h=NH)
        pT = zs(O_PT, 2304).rearrange("p (h n) -> p h n", h=NH)
        qkv = zf(O_QKV, 2304).rearrange("p (c t) -> p c t", c=9)
        zt = zf(O_Z, 768).rearrange("p (b n) -> p b n", b=2)
        cin = zf(O_CIN, 9 * 259).rearrange("p (c t) -> p c t", c=9)
        sq = zs(O_SQ, 1536).rearrange("p (c t) -> p c t", c=6)
        rn = zs(O_RN, 1536).rearrange("p (c t) -> p c t", c=6)

        def by_pair(o):
            return zs(o, 1536).rearrange("p (i c) -> p i c", i=12)

        tg, dt_, U, Tm, A = by_pair(O_TG), by_pair(O_DT), by_pair(O_U), by_pair(O_T), by_pair(O_A)
        M = [by_pair(O_MM), by_pair(O_MM + 1536)]
        LA = zs(O_LA, 3072).rearrange("p (i w c) -> p i w c", i=12, w=2)
        kv = zf(O_KV, 1536).rearrange("p (w b n) -> p w b n", w=2, b=2)
        kg = zf(O_KG, 768).rearrange("p (b n) -> p b n", b=2)
        kd = zf(O_KD, 768).rearrange("p (b n) -> p b n", b=2)
        up = zf(O_UP, 768).rearrange("p (b n) -> p b n", b=2)
        wT = zf(O_WT, 768).rearrange("p (j t) -> p j t", j=3)
        vp = zf(O_VP, 768).rearrange("p (b n) -> p b n", b=2)
        o = zf(O_O, 768).rearrange("p (b n) -> p b n", b=2)
        S = zf(O_ST, 384).rearrange("p (j e) -> p j e", j=3)
        osq = up
        sg = [zf(O_SG + 512 * i, 512) for i in range(2)]
        hh = [zf(O_H + 512 * i, 512) for i in range(2)]
        hT = [zf(O_HT + 512 * i, 512).rearrange("p (k t) -> p k t", k=4) for i in range(2)]
        xg = zf(O_XG, 1024).rearrange("p (k t) -> p k t", k=KT)
        pick = zf(O_P, 256).rearrange("p (b s) -> p b s", b=2)
        pickw = zf(O_PW, 256).rearrange("p (b s) -> p b s", b=2)
        pwT = zf(O_PWT, 256)
        ye = zf(O_YE, 1024)
        fa = zf(O_FA, 2048).rearrange("p (b d) -> p b d", b=2)

        def sm(a, n):
            return small[:, a:a + n]

        ab = sm(0, 24).rearrange("p (b c) -> p b c", b=2)
        xx, l1, beta, g_i, gsum = sm(24, 12), sm(36, 12), sm(48, 12), sm(60, 12), sm(72, 48)
        eg, ekl, eS, ngc, rsum, rinv = sm(120, 12), sm(132, 12), sm(144, 24), sm(168, 12), sm(180, 12), sm(192, 12)
        nmax, ss = sm(204, 12), sm(216, 12)
        stats, mvar, rstd = sm(228, 12), sm(240, 2), sm(242, 1)
        nA = sm(244, 12)
        std = sb("std", 4)
        gbh = sb("gbh", 4)

        def by_bh(t):
            return t.rearrange("p (r j b) -> p b j r", r=2, j=3)

        slot_loaded = [sem(f"slot_loaded_{s}") for s in range(NSLOT)]
        wo_used = sem("wo_used")
        x_loaded, cst_loaded, par_loaded, b_loaded, glu_loaded, ln_loaded = (
            sem(n) for n in ("x_loaded", "cst_loaded", "par_loaded", "b_loaded", "glu_loaded", "ln_loaded"))
        x_ready, xt_psum, xt_act, xt_dve = (sem(n) for n in ("x_ready", "xt_psum", "xt_act", "xt_dve"))
        proj_psum, proj_evac = sem("proj_psum"), sem("proj_evac")
        s5_step, s5_reduced, s5_sines = sem("s5_step"), sem("s5_reduced"), sem("s5_sines")
        phase_ready, c_ready = sem("phase_ready"), sem("c_ready")
        s5_params = sem("s5_params")
        bu_psum, bu_used, states_ready = sem("bu_psum"), sem("bu_used"), sem("states_ready")
        y_psum, y_sum, y_gelu, glu_psum, glu_sig = (sem(n) for n in ("y_psum", "y_sum", "y_gelu", "glu_psum",
                                                                      "glu_sig"))
        glu_bias = sem("glu_bias")
        sc_psum, sc_evac, sc_max, sc_exp, sc_norm = (sem(n) for n in ("sc_psum", "sc_evac", "sc_max", "sc_exp",
                                                                       "sc_norm"))
        pt_psum, pt_evac, pv_psum, pv_evac = (sem(n) for n in ("pt_psum", "pt_evac", "pv_psum", "pv_evac"))
        conv_done, silu_done, sq_done = sem("conv_done"), sem("silu_done"), sem("sq_done")
        nrm_psum, nrm_sqrt, qk_ready = sem("nrm_psum"), sem("nrm_sqrt"), sem("qk_ready")
        gate_in, gate_ln, gate_tanh, g_ready, tg_ready = (sem(n) for n in ("gate_in", "gate_ln", "gate_tanh",
                                                                            "g_ready", "tg_ready"))
        nA_exp = sem("nA_exp")
        gs_psum, gs_evac, gs_dve, gs_exp, kd_ready = (sem(n) for n in ("gs_psum", "gs_evac", "gs_dve", "gs_exp",
                                                                        "kd_ready"))
        gb_psum, gb_evac, dt_exp = sem("gb_psum"), sem("gb_evac"), sem("dt_exp")
        kv_psum, kv_evac = sem("kv_psum"), sem("kv_evac")
        kk_psum, la_ready, m_ready = sem("kk_psum"), sem("la_ready"), sem("m_ready")
        u_ready, t_psum, t_ready = sem("u_ready"), sem("t_psum"), sem("t_ready")
        a_psum, a_evac, xy_psum, xy_used = (sem(n) for n in ("a_psum", "a_evac", "xy_psum", "xy_used"))
        up_psum_, up_evac, w_psum, w_evac = (sem(n) for n in ("up_psum", "up_evac", "w_psum", "w_evac"))
        s_zero, ws_psum, qs_psum, vp_ready, su_psum, s_ready, qs_used = (
            sem(n) for n in ("s_zero", "ws_psum", "qs_psum", "vp_ready", "su_psum", "s_ready", "qs_used"))
        av_psum, o_ready, o_sq, o_ss, o_std, og_ready, zw_ready = (
            sem(n) for n in ("av_psum", "o_ready", "o_sq", "o_ss", "o_std", "og_ready", "zw_ready"))
        ot_psum, mix_ready = sem("ot_psum"), sem("mix_ready")
        res_psum, ln_var, ln_std = sem("res_psum"), sem("ln_var"), sem("ln_std")
        gate_psum, up_psum, gate_silu, h_ready, ht_psum, ht_evac, down_done = (
            sem(n) for n in ("gate_psum", "uppr_psum", "gate_silu", "h_ready", "ht_psum", "ht_evac", "down_done"))
        lg_psum, gate_exp_in, gate_exp, sel_ready, pos_psum, route_ready = (
            sem(n) for n in ("lg_psum", "gate_exp_in", "gate_exp", "sel_ready", "pos_psum", "route_ready"))
        pick_ready, pickw_ready, pwt_psum, pwt_evac = (
            sem(n) for n in ("pick_ready", "pickw_ready", "pwt_psum", "pwt_evac"))
        xg_psum, xg_act, xg_dve, ye_act, ye_dve, sc_out, sc_added = (
            sem(n) for n in ("xg_psum", "xg_act", "xg_dve", "ye_act", "ye_dve", "scatter_psum",
                             "scatter_added"))
        out_ready, out_stored = sem("out_ready"), sem("out_stored")
        dve_step, act_step, pool_step = sem("dve_step"), sem("act_step"), sem("pool_step")

        DENSE_UNITS = NB * FC

        class Order:

            def __init__(self, eng, s):
                self.eng, self.s, self.n = eng, s, 0

            def __call__(self, ins):
                ins.then_inc(self.s, 1)
                self.n += 1

            def wait(self):
                if self.n:
                    self.eng.wait_ge(self.s, self.n)

            def then(self, ins):
                self(ins)
                self.wait()

        def in_chunk(l, c):
            c0, n = WIN[c]
            return w_in[l].rearrange("(k p) n -> p k n", p=P)[:, :, c0:c0 + n], KT * n

        def wide(w, j):
            return w.rearrange("(k p) f -> p k f", p=P)[:, :, 512 * j:512 * (j + 1)]

        def tall(w, j):
            return w.rearrange("(k p) n -> p k n", p=P)[:, 4 * j:4 * (j + 1), :]

        def slot_wide(s, n=512):
            return slot(s)[:, 0:KT * n].rearrange("p (k n) -> p k n", k=KT)

        def slot_tall(s):
            return slot(s)[:, 0:4096].rearrange("p (k n) -> p k n", k=4)

        block = ctx.enter_context(nc.Block())

        @block.sync
        def _(sp):
            def wait_used(m):
                l = int(m >= FIRST[1])
                c = m - FIRST[l]
                if c < 6:
                    sp.wait_ge(proj_psum, 13 * l + (2, 4, 6, 8, 10, 13)[c])
                elif c == 6:
                    sp.wait_ge(wo_used, l + 1)
                elif c == 7:
                    sp.wait_ge(res_psum, 6 * l + 4)
                else:
                    j, w = divmod(c - PER_LAYER, 3)
                    sp.wait_ge((gate_psum, up_psum, down_done)[w], NB * (j + 1))

            def load(m, dst, src):
                if m >= SLOTS:
                    wait_used(m - SLOTS)
                sp.dma_start(dst, src).then_inc(slot_loaded[m % SLOTS], 16)

            sp.dma_start(x[:, 0, :], x_in[0, 0:P, :]).then_inc(x_loaded, 16)
            sp.dma_start(x[:, 1, :], x_in[0, P:T, :]).then_inc(x_loaded, 16)
            for l in range(L):
                m = FIRST[l]
                for c in range(len(WIN)):
                    load(m + c, slot_wide((m + c) % SLOTS, WIN[c][1]), in_chunk(l, c)[0])
                for c in range(2):
                    load(m + 6 + c, slot_tall((m + 6 + c) % SLOTS), tall(w_out[l], c))
                if l == 0:
                    for j in range(FC):
                        for w, (src, kind) in enumerate(((wg, wide), (wu, wide), (wd, tall))):
                            n = m + PER_LAYER + 3 * j + w
                            dst = slot_wide(n % SLOTS) if w < 2 else slot_tall(n % SLOTS)
                            load(n, dst, kind(src[0], j))

            def expert_chunk(e, r):
                j, w = divmod(r, 3)
                src = (mg, mu, md)[w][0, bass.ds(e, 1)].rearrange("one a b -> (one a) b")
                dst = slot_wide(r % NSLOT) if w < 2 else slot_tall(r % NSLOT)
                sp.dma_start(dst, wide(src, j) if w < 2 else tall(src, j)).then_inc(slot_loaded[r % NSLOT], 16)

            for r in range(NSLOT):
                if r < SLOTS:
                    wait_used(max(m for m in range(N_PRE) if m % SLOTS == r))
                elif r == SLOTS:
                    sp.wait_ge(x_ready, 5)
                expert_chunk(0, r)

            def wait_expert_used(i, r):
                j, w = divmod(r, 3)
                sp.wait_ge((gate_psum, up_psum, down_done)[w], i * FC + (DENSE_UNITS + j + 1))

            def stream(first):
                with sp.Fori(first, first + NE - 1) as i:
                    for r in range(NSLOT, EXP):
                        wait_expert_used(i, r - NSLOT)
                        expert_chunk(i - first, r)
                    for r in range(NSLOT):
                        wait_expert_used(i, r + EXP - NSLOT)
                        expert_chunk(i - (first - 1), r)
                for r in range(NSLOT, EXP):
                    wait_expert_used(first + NE - 1, r - NSLOT)
                    expert_chunk(NE - 1, r)

            stream(0)
            sp.wait_ge(route_ready, 1)
            most = sp.value_load(count_i[0:1, 0:1], min_val=0, max_val=T)
            with sp.If(most > P):
                for r in range(NSLOT):
                    wait_expert_used(NE - 1, r + EXP - NSLOT)
                    expert_chunk(0, r)
                stream(NE)
            for b in range(NB):
                sp.wait_ge(out_ready, b + 1)
                sp.dma_start(out[0, b * P:(b + 1) * P, :], x[:, b, :]).then_inc(out_stored, 16)
            sp.wait_ge(out_stored, 16 * NB)

        def phase_table(eng, step, l):
            tt = eng.tensor_tensor
            pr, pi, qr, qi, t0, t1 = (s5s[:, (12 + k) * 16 + 8 * l:(12 + k) * 16 + 8 * l + 8] for k in range(6))
            step(eng.memset(cos_t[:, :, 0:1], 1.0))
            step(eng.memset(sin_t[:, :, 0:1], 0.0))
            step.wait()
            cur, nxt = (pr, pi), (qr, qi)
            k = 1
            tmp = zone_s[:, O_BP:O_BP + 2048] if l else zone_s[:, O_M:O_M + 2048]
            while k < T:
                a = tmp[:, 0:ST * k].rearrange("p (j t) -> p j t", j=ST)
                b = tmp[:, 1024:1024 + ST * k].rearrange("p (j t) -> p j t", j=ST)
                cb = cur[0].unsqueeze(2).to_broadcast([P, ST, k])
                sb_ = cur[1].unsqueeze(2).to_broadcast([P, ST, k])
                step(tt(a, cos_t[:, :, 0:k], cb, ALU.mult))
                step(tt(b, sin_t[:, :, 0:k], sb_, ALU.mult))
                step.wait()
                step(tt(cos_t[:, :, k:2 * k], a, b, ALU.subtract))
                step.wait()
                step(tt(a, cos_t[:, :, 0:k], sb_, ALU.mult))
                step(tt(b, sin_t[:, :, 0:k], cb, ALU.mult))
                if 2 * k < T:
                    step(tt(t0, cur[0], cur[0], ALU.mult))
                    step(tt(t1, cur[1], cur[1], ALU.mult))
                    step(tt(nxt[1], cur[0], cur[1], ALU.mult))
                    step.wait()
                    step(tt(nxt[0], t0, t1, ALU.subtract))
                    step(eng.tensor_scalar(nxt[1], nxt[1], 2.0, None, ALU.mult))
                step.wait()
                last = tt(sin_t[:, :, k:2 * k], a, b, ALU.add)
                if 2 * k < T:
                    step(last)
                    step.wait()
                cur, nxt = nxt, cur
                k *= 2
            last.then_inc(phase_ready, 1)

        @block.gpsimd
        def _(pool):
            step = Order(pool, pool_step)
            pool.dma_start(cst[:, :], consts).then_inc(cst_loaded, 16)
            pool.dma_start(par[:, :], params).then_inc(par_loaded, 16)
            pool.dma_start(b_pad, s5_b[0]).then_inc(b_loaded, 16)
            pool.dma_start(gw, glu_w[0]).then_inc(glu_loaded, 16)
            for l in range(L):
                if l:
                    pool.wait_ge(x_ready, 1)
                    pool.wait_ge(s5_params, 1)
                    phase_table(pool, step, l)
                    pool.wait_ge(phase_ready, l + 1)
                    pool.dma_start(b_pad, s5_b[1]).then_inc(b_loaded, 16)
                    pool.dma_start(gw, glu_w[1]).then_inc(glu_loaded, 16)
                pool.wait_ge(pt_psum, NH * (l + 1))
                pool.dma_start(lnrow, ln[2 * l].partition_broadcast(P)).then_inc(ln_loaded, 16)
                for v in range(6):
                    if v == 0:
                        pool.wait_ge(la_ready, 6 * (l + 1))
                    if v == 2:
                        pool.wait_ge(t_psum, 3 * (l + 1))
                        pool.wait_ge(u_ready, l + 1)
                    if v > 2:
                        pool.wait_ge(a_psum, 15 * l + 3 * (v - 2))
                    pool.tensor_tensor(M[v % 2], LA[:, :, 1, :],
                                       C(f"lv{v}").unsqueeze(1).to_broadcast([P, 12, P]), ALU.mult)\
                        .then_inc(m_ready, 1)
                pool.wait_ge(x_ready, 2 * NB * l + NB)
                pool.dma_start(lnrow, ln[2 * l + 1].partition_broadcast(P)).then_inc(ln_loaded, 16)

        @block.scalar
        def _(act):
            af = nc.scalar.activation
            step = Order(act, act_step)
            for l in range(L):
                n_x = 2 * l
                for q in range(2):
                    act.wait_ge(xt_psum, 4 * n_x + q + 1)
                    af(xT[:, 2 * q:2 * q + 2, :], ps[:, q, :], ACT.Copy).then_inc(xt_act, 1)
                if l == 0:
                    act.wait_ge(par_loaded, 16)
                    af(s5s[:, 0:16], par[:, PO["ldt"]:PO["ldt"] + 16], ACT.Exp).then_inc(s5_step, 1)
                    af(nA, par[:, PO["alog"]:PO["alog"] + 12], ACT.Exp).then_inc(nA_exp, 1)
                    act.wait_ge(cst_loaded, 16)
                    act.wait_ge(s5_reduced, 1)
                    af(s5s[:, 32:48], s5s[:, 64:80], ACT.Sin).then_inc(s5_sines, 1)
                    af(s5s[:, 48:64], s5s[:, 80:96], ACT.Sin, bias=cst[:, C_HPI:C_HPI + 1], scale=-1.0)\
                        .then_inc(s5_sines, 1)

                def evac(n, *pairs):
                    act.wait_ge(proj_psum, 13 * l + n + 1)
                    for k, (dst, src) in enumerate(pairs):
                        ins = af(dst, src, ACT.Copy)
                        if k == len(pairs) - 1:
                            ins.then_inc(proj_evac, 1)
                        else:
                            step(ins)

                if l:
                    act.wait_ge(x_ready, 4)
                evac(0, (uT, ps[:, 4, :]))
                evac(1, (qkm[:, 0:2, :], ps[:, 5, :]))
                evac(2, (qkm[:, 2:4, :], ps[:, 2, :]))
                evac(3, (qkm[:, 4:6, :], ps[:, 3, :]))
                evac(4, (mv[:, 0, :], ps[:, 4, 0:384]))
                evac(5, (mv[:, 1, :], ps[:, 5, 0:384]))
                evac(6, (cin[:, 0:2, 3:259], ps[:, 6, :].rearrange("p (a t) -> p a t", a=2)))
                evac(7, (cin[:, 2:4, 3:259], ps[:, 7, :].rearrange("p (a t) -> p a t", a=2)))
                act.wait_ge(sc_max, l + 1)
                for h in range(NH):
                    for b, (c0, n) in enumerate(((0, P), (P, T))):
                        af(sc[:, h, c0:c0 + n], sc[:, h, c0:c0 + n], ACT.Exp, bias=nmax[:, 6 * b + h:6 * b + h + 1],
                           accum_out=rsum[:, 6 * b + h:6 * b + h + 1]).then_inc(sc_exp, 1)
                evac(8, (cin[:, 4:6, 3:259], ps[:, 0, :].rearrange("p (a t) -> p a t", a=2)))
                evac(9, (cin[:, 6:8, 3:259], ps[:, 1, :].rearrange("p (a t) -> p a t", a=2)))
                evac(10, (cin[:, 8, 3:259], ps[:, 4, 0:T]))
                for b, bank in ((0, 5), (1, 2)):
                    act.wait_ge(proj_psum, 13 * l + 12 + b)
                    step(af(ab[:, b, :], ps[:, bank, 384:396], ACT.Copy))
                    af(zt[:, b, :], ps[:, bank, 0:384], ACT.Silu).then_inc(proj_evac, 1)
                for c in range(3):
                    act.wait_ge(conv_done, 3 * l + c + 1)
                    af(qkv[:, 3 * c:3 * c + 3, :], qkv[:, 3 * c:3 * c + 3, :], ACT.Silu).then_inc(silu_done, 1)
                act.wait_ge(silu_done, 3 * l + 2)
                act.wait_ge(states_ready, 2 * (l + 1))
                af(sq, qkv[:, 0:6, :], ACT.Square).then_inc(sq_done, 1)
                act.wait_ge(gate_in, l + 1)
                af(l1, l1, ACT.Exp, scale=-1.0).then_inc(gate_ln, 1)
                act.wait_ge(gate_ln, 2 * l + 1)
                af(l1, l1, ACT.Ln, bias=cst[:, C_ONE:C_ONE + 1]).then_inc(gate_ln, 1)
                act.wait_ge(proj_evac, 13 * (l + 1))
                af(by_bh(beta), ab[:, :, 6:12].rearrange("p b (j r) -> p b j r", j=3), ACT.Tanh, scale=0.5)\
                    .then_inc(gate_tanh, 1)
                act.wait_ge(y_sum, l + 1)
                af(ys, ys, ACT.Gelu_apprx_tanh).then_inc(y_gelu, 1)
                act.wait_ge(glu_psum, l + 1)
                act.wait_ge(glu_bias, 1)
                for f in range(2):
                    af(sig[:, f, :], ps[:, 6, f * T:(f + 1) * T], ACT.Tanh, bias=gbh[:, 2 * l + f:2 * l + f + 1],
                       scale=0.5).then_inc(glu_sig, 1)
                for h in range(NH):
                    act.wait_ge(pt_psum, NH * l + h + 1)
                    af(pT[:, h, :], ps[:, (7, 0)[h % 2], 0:384], ACT.Copy).then_inc(pt_evac, 1)
                act.wait_ge(gs_psum, l + 1)
                af(gsum, ps[:, 5, 0:48], ACT.Copy).then_inc(gs_evac, 1)
                act.wait_ge(gs_evac, l + 1)
                af(eg, gsum[:, 0:12], ACT.Exp).then_inc(gs_exp, 1)
                af(eS, gsum[:, 24:48], ACT.Exp).then_inc(gs_exp, 1)
                act.wait_ge(gs_dve, l + 1)
                af(ekl, ekl, ACT.Exp).then_inc(gs_exp, 1)
                for q, bank in enumerate((2, 3, 6)):
                    act.wait_ge(nrm_psum, 3 * l + q + 1)
                    af(rn[:, 2 * q:2 * q + 2, :], ps[:, bank, :], ACT.Sqrt, bias=cst[:, C_EPS6:C_EPS6 + 1])\
                        .then_inc(nrm_sqrt, 1)
                act.wait_ge(gb_evac, 3 * (l + 1))
                for i in range(12):
                    af(dt_[:, i, :], dt_[:, i, :], ACT.Exp, bias=ngc[:, i:i + 1]).then_inc(dt_exp, 1)
                for q, bank in enumerate((4, 5, 2)):
                    act.wait_ge(kv_psum, 3 * l + q + 1)
                    dst = zf(O_KV + 512 * q, 512)
                    af(dst, ps[:, bank, :], ACT.Copy).then_inc(kv_evac, 1)
                for n in range(15):
                    act.wait_ge(a_psum, 15 * l + n + 1)
                    g = n % 3
                    if n >= 3:
                        act.wait_ge(xy_psum, 15 * l + n - 2)
                    af(A[:, 4 * g:4 * g + 4, :], ps[:, (2, 5)[n % 2], :], ACT.Copy).then_inc(a_evac, 1)
                for q in range(2):
                    act.wait_ge(w_psum, 2 * l + q + 1)
                    af(wT[:, 2 * q:2 * q + 2 - q, :], ps[:, q, 0:512 - 256 * q], ACT.Copy).then_inc(w_evac, 1)
                for b in range(NB):
                    act.wait_ge(o_ready, NB * l + b + 1)
                    af(osq[:, b, :], o[:, b, :], ACT.Square).then_inc(o_sq, 1)
                    act.wait_ge(o_ss, NB * l + b + 1)
                    af(ss[:, 6 * b:6 * b + 6], ss[:, 6 * b:6 * b + 6], ACT.Sqrt, bias=cst[:, C_EPS6:C_EPS6 + 1],
                       scale=1.0 / HD).then_inc(o_std, 1)

                def norm(n):
                    for b in range(NB):
                        act.wait_ge(ln_var, NB * n + b + 1)
                        af(std[:, b:b + 1], mvar[:, 1:2], ACT.Sqrt, bias=cst[:, C_EPS5:C_EPS5 + 1])\
                            .then_inc(ln_std, 1)

                norm(2 * l)
                for q in range(2):
                    act.wait_ge(xt_psum, 4 * (n_x + 1) + q + 1)
                    af(xT[:, 2 * q:2 * q + 2, :], ps[:, (4, 3)[q], :], ACT.Copy).then_inc(xt_act, 1)
                if l == 0:
                    for u in range(DENSE_UNITS):
                        act.wait_ge(gate_psum, u + 1)
                        if u >= 2:
                            act.wait_ge(h_ready, u - 1)
                        af(sg[u % 2], ps[:, 4, :], ACT.Silu).then_inc(gate_silu, 1)
                        if u >= 1:
                            v = u - 1
                            act.wait_ge(ht_psum, v + 1)
                            if v >= 2:
                                act.wait_ge(down_done, v - 1)
                            af(hT[v % 2], ps[:, 6 + v % 2, :], ACT.Copy).then_inc(ht_evac, 1)
                    v = DENSE_UNITS - 1
                    act.wait_ge(ht_psum, v + 1)
                    act.wait_ge(down_done, v - 1)
                    af(hT[v % 2], ps[:, 6 + v % 2, :], ACT.Copy).then_inc(ht_evac, 1)
                    norm(1)
            act.wait_ge(gate_exp_in, 1)
            af(rt[:, 100:102], rt[:, 98:100], ACT.Exp).then_inc(gate_exp, 1)

            def gathered(n):
                act.wait_ge(xg_psum, n)
                af(xg[:, 0:4, :], ps[:, 2, :], ACT.Copy).then_inc(xg_act, 1)

            def expert(i):
                u0 = i * FC + DENSE_UNITS

                def evac_h(j):
                    act.wait_ge(ht_psum, u0 + (j + 1))
                    act.wait_ge(down_done, u0 + max(j - 1, 0))
                    af(hT[j % 2], ps[:, 6 + j % 2, :], ACT.Copy).then_inc(ht_evac, 1)

                for j in range(FC):
                    act.wait_ge(gate_psum, u0 + (j + 1))
                    act.wait_ge(h_ready, u0 + max(j - 1, 0))
                    af(sg[j % 2], ps[:, 4, :], ACT.Silu).then_inc(gate_silu, 1)
                    if j >= 1:
                        evac_h(j - 1)
                gathered(i * 2 + 3)
                evac_h(FC - 1)
                act.wait_ge(down_done, u0 + FC)
                af(ye[:, 0:512], ps[:, 0, :], ACT.Copy).then_inc(ye_act, 1)

            act.wait_ge(xt_psum, 16)
            gathered(1)
            with act.Fori(0, NE) as i:
                expert(i)
            act.wait_ge(route_ready, 1)
            most = act.value_load(count_i[0:1, 0:1], min_val=0, max_val=T)
            with act.If(most > P):
                with act.Fori(NE, 2 * NE) as i:
                    expert(i)
            for b in range(NB):
                act.wait_ge(ln_var, NB * 3 + b + 1)
                af(std[:, b:b + 1], mvar[:, 1:2], ACT.Sqrt, bias=cst[:, C_EPS5:C_EPS5 + 1]).then_inc(ln_std, 1)

        @block.vector
        def _(dve):
            v_ = nc.vector
            tt, ts, stt = v_.tensor_tensor, v_.tensor_scalar, v_.scalar_tensor_tensor
            step = Order(dve, dve_step)

            def pc(name, l, n):
                return par[:, PO[name] + l * n:PO[name] + (l + 1) * n]

            def s5_parameters():
                N = L * ST
                sv = [s5s[:, N * k:N * (k + 1)] for k in range(24)]
                st, _, sh, ch, half, ahalf, a, th, w, e, k_, t0, pr, pi, _, _, t1, t2 = sv[:18]
                fr, fi, rad, den, xr, xi = sv[18:24]
                lre, lim = par[:, PO["lre"]:PO["lre"] + N], par[:, PO["lim"]:PO["lim"] + N]
                dve.wait_ge(s5_step, 1)
                step(tt(a, lre, st, ALU.mult))
                step.then(tt(th, lim, st, ALU.mult))
                big = 1.5 * 2.0 ** 23
                step.then(ts(k_, th, float(1 / (2 * np.pi)), big, ALU.mult, ALU.add))
                step.then(ts(k_, k_, -big, None, ALU.add))
                c1 = 6.28125
                c2 = float(np.float32(np.floor((2 * np.pi - c1) * 2 ** 20) / 2 ** 20))
                c3 = float(2 * np.pi - c1 - c2)
                for c in (c1, c2, c3):
                    step.then(stt(th, k_, -c, th, ALU.mult, ALU.add))
                step.then(ts(half, th, 0.5, float(np.float32(1.5707963)), ALU.mult, ALU.min))
                step.then(ts(half, half, -float(np.float32(1.5707963)), None, ALU.max))
                stt(ahalf, half, -1.0, half, ALU.mult, ALU.max).then_inc(s5_reduced, 1)
                step.then(ts(w, a, -100.0, 88.0, ALU.max, ALU.min))
                step.then(ts(w, w, 1.0 / 128, None, ALU.mult))
                fact = 3628800.0
                step.then(ts(e, w, 1.0 / fact, None, ALU.mult))
                for n in range(9, 0, -1):
                    fact = fact / (n + 1)
                    step.then(stt(e, e, 1.0 / fact, w, ALU.add, ALU.mult))
                for _i in range(7):
                    step.then(stt(e, e, 2.0, e, ALU.add, ALU.mult))
                step(ts(rad, e, 1.0, None, ALU.add))
                dve.wait_ge(s5_sines, 2)
                step.then(tt(t0, sh, sh, ALU.mult))
                step.then(ts(t0, t0, -2.0, None, ALU.mult))
                step(ts(pr, t0, 1.0, None, ALU.add))
                step.then(stt(pi, sh, 2.0, ch, ALU.mult, ALU.mult))
                step.then(tt(t1, e, pr, ALU.mult))
                step(tt(xr, t1, t0, ALU.add))
                step.then(tt(xi, rad, pi, ALU.mult))
                step(tt(t1, lre, lre, ALU.mult))
                step.then(tt(t2, lim, lim, ALU.mult))
                step.then(tt(den, t1, t2, ALU.add))
                step.then(v_.reciprocal(den, den))
                step(tt(t1, xr, lre, ALU.mult))
                step.then(tt(t2, xi, lim, ALU.mult))
                step.then(tt(t1, t1, t2, ALU.add))
                step.then(tt(fr, t1, den, ALU.mult))
                step(tt(t1, xi, lre, ALU.mult))
                step.then(tt(t2, xr, lim, ALU.mult))
                step.then(tt(t1, t1, t2, ALU.subtract))
                tt(fi, t1, den, ALU.mult).then_inc(s5_params, 1)
                dve.wait_ge(s5_params, 1)
                ts(gbh[:, :], par[:, PO["gb"]:PO["gb"] + 4], 0.5, None, ALU.mult).then_inc(glu_bias, 1)
                dve.wait_ge(nA_exp, 1)
                step.then(ts(nA, nA, -1.0, None, ALU.mult))

            def c_padded(l):
                cc = par[:, PO["c"] + 256 * l:PO["c"] + 256 * (l + 1)].rearrange("p (j r f) -> p j r f", j=ST, r=2)
                fr, fi = (s5s[:, 16 * k + 8 * l:16 * k + 8 * l + 8].unsqueeze(2).to_broadcast([P, ST, 16])
                          for k in (18, 19))
                t = [mt[0][:, 128 * k:128 * (k + 1)].rearrange("p (j f) -> p j f", j=ST) for k in range(4)]
                step(v_.memset(c_pad, 0.0))
                step(tt(t[0], cc[:, :, 0, :], fr, ALU.mult))
                step(tt(t[1], cc[:, :, 1, :], fi, ALU.mult))
                step(tt(t[2], cc[:, :, 1, :], fr, ALU.mult))
                step.then(tt(t[3], cc[:, :, 0, :], fi, ALU.mult))
                for half in range(2):
                    rows = slice(64 * half, 64 * half + 64)
                    for q in range(4):
                        f0 = 32 * q + 16 * half
                        step(tt(c_pad[rows, q::4, 0, f0:f0 + 16], t[0][rows, q::4], t[1][rows, q::4], ALU.subtract))
                        ins = stt(c_pad[rows, q::4, 1, f0:f0 + 16], t[2][rows, q::4], -1.0, t[3][rows, q::4],
                                  ALU.mult, ALU.subtract)
                        if (half, q) != (1, 3):
                            step(ins)
                ins.then_inc(c_ready, 1)
                dve.wait_ge(c_ready, l + 1)
                step.wait()

            def s5_scan(l, t):
                re, im = ((6, 0), (4, 2))[t]
                cs = cos_t[:, 4 * t:4 * t + 4, :].rearrange("p (a j) t -> p a (j t)", a=2)
                sn = sin_t[:, 4 * t:4 * t + 4, :].rearrange("p (a j) t -> p a (j t)", a=2)
                v3 = [m.rearrange("p (a n) -> p a n", a=2) for m in mt]
                out_s = [states[r][:, 4 * t:4 * t + 4, :].rearrange("p (a j) t -> p a (j t)", a=2) for r in range(2)]
                dve.wait_ge(bu_psum, 2 * l + t + 1)
                step(tt(v3[0], ps[:, re:re + 2, :], cs, ALU.mult))
                step(tt(v3[1], ps[:, im:im + 2, :], sn, ALU.mult))
                step(tt(v3[2], ps[:, im:im + 2, :], cs, ALU.mult))
                tt(v3[3], ps[:, re:re + 2, :], sn, ALU.mult).then_inc(bu_used, 1)
                dve.wait_ge(bu_used, 2 * l + t + 1)
                step.wait()
                step(tt(mt[0], mt[0], mt[1], ALU.add))
                step.then(tt(mt[2], mt[2], mt[3], ALU.subtract))
                for jj in range(4):
                    r0 = 16 * 20 + 8 * l + 4 * t + jj
                    rad = s5s[:, r0:r0 + 1].to_broadcast([P, T])
                    for k in range(2):
                        step(v_.tensor_tensor_scan(mt[2 * k + 1][:, jj * T:(jj + 1) * T], rad,
                                                   mt[2 * k][:, jj * T:(jj + 1) * T], 0.0, ALU.mult, ALU.add))
                step.wait()
                step(tt(v3[0], v3[1], cs, ALU.mult))
                step(tt(v3[2], v3[3], sn, ALU.mult))
                step.wait()
                step(tt(out_s[0], v3[0], v3[2], ALU.subtract))
                step.wait()
                step(tt(v3[0], v3[3], cs, ALU.mult))
                step(tt(v3[2], v3[1], sn, ALU.mult))
                step.wait()
                tt(out_s[1], v3[0], v3[2], ALU.add).then_inc(states_ready, 1)
                dve.wait_ge(states_ready, 2 * l + t + 1)

            def norm(n, banks, sum_of):
                for b in range(NB):
                    dve.wait_ge(ln_loaded, 16 * (n + 1))
                    for c in range(2):
                        xc = x[:, b, 512 * c:512 * (c + 1)]
                        if banks is not None:
                            sum_of(b, c)
                            add = ps[:, banks[2 * b + c], :]
                        else:
                            add = fa[:, b, 512 * c:512 * (c + 1)]
                        step.then(stt(xc, xc, ALPHA, add, ALU.mult, ALU.add))
                        step(v_.bn_stats(stats[:, 6 * c:6 * c + 6], xc))
                    step.wait()
                    if b:
                        dve.wait_ge(ln_std, NB * n + b)
                    v_.bn_aggr(mvar, stats).then_inc(ln_var, 1)
                    dve.wait_ge(ln_var, NB * n + b + 1)
                    step.then(stt(x[:, b, :], x[:, b, :], mvar[:, 0:1], lnrow[:, 0, :], ALU.subtract, ALU.mult))
                    dve.wait_ge(ln_std, NB * n + b + 1)
                    step.then(v_.reciprocal(rstd, std[:, b:b + 1]))
                    s_done = out_ready if n == 3 else x_ready
                    stt(x[:, b, :], x[:, b, :], rstd, lnrow[:, 1, :], ALU.mult, ALU.add).then_inc(s_done, 1)
                    dve.wait_ge(s_done, (0 if n == 3 else NB * n) + b + 1)

            def x_transposed(n, banks):
                for q in range(2, 4):
                    dve.wait_ge(xt_psum, 4 * n + q + 1)
                    v_.tensor_copy(xT[:, 2 * q:2 * q + 2, :], ps[:, banks[q], :]).then_inc(xt_dve, 1)

            dve.wait_ge(cst_loaded, 16)
            dve.wait_ge(par_loaded, 16)
            for l in range(L):
                x_transposed(2 * l, (0, 1, 6, 7))
                if l == 0:
                    s5_parameters()
                    phase_table(v_, step, 0)
                    dve.wait_ge(phase_ready, 1)
                else:
                    dve.wait_ge(phase_ready, 2)
                c_padded(l)
                step(v_.memset(cin[:, :, 0:3], 0.0))
                s5_scan(l, 0)
                for h in range(NH):
                    bank = (2, 3, 6, 7, 0, 1)[h]
                    dve.wait_ge(sc_psum, NH * l + h + 1)
                    step(stt(sc[:, h, 0:P], ps[:, bank, 0:P], SCALE, C("causal"), ALU.mult, ALU.add))
                    step(ts(sc[:, h, P:2 * P], ps[:, bank, P:2 * P], SCALE, None, ALU.mult))
                    stt(sc[:, h, 2 * P:3 * P], ps[:, bank, 2 * P:3 * P], SCALE, C("causal"), ALU.mult, ALU.add)\
                        .then_inc(sc_evac, 1)
                dve.wait_ge(sc_evac, NH * (l + 1))
                step.wait()
                step(v_.tensor_reduce(nmax[:, 0:6], sc[:, :, 0:P], AX_X, ALU.max))
                step.then(v_.tensor_reduce(nmax[:, 6:12], sc[:, :, P:3 * P], AX_X, ALU.max))
                ts(nmax, nmax, -1.0, None, ALU.mult).then_inc(sc_max, 1)
                s5_scan(l, 1)
                dve.wait_ge(sc_exp, 2 * NH * (l + 1))
                step.then(v_.reciprocal(rinv, rsum))
                for b, (c0, n) in enumerate(((0, P), (P, T))):
                    tt(sc[:, :, c0:c0 + n], sc[:, :, c0:c0 + n],
                       rinv[:, 6 * b:6 * b + 6].unsqueeze(2).to_broadcast([P, NH, n]), ALU.mult)\
                        .then_inc(sc_norm, 1)
                cw = par[:, PO["conv"] + 36 * l:PO["conv"] + 36 * (l + 1)].rearrange("p (c w) -> p c w", c=9)
                for c in range(9):
                    if c % 2 == 0:
                        dve.wait_ge(proj_evac, 13 * l + 7 + c // 2)
                    step.then(ts(qkv[:, c, :], cin[:, c, 0:T], cw[:, c, 0:1], None, ALU.mult))
                    for w in range(1, 4):
                        ins = stt(qkv[:, c, :], cin[:, c, w:w + T], cw[:, c, w:w + 1], qkv[:, c, :],
                                  ALU.mult, ALU.add)
                        if w == 3 and c % 3 == 2:
                            ins.then_inc(conv_done, 1)
                        else:
                            step.then(ins)
                dve.wait_ge(proj_evac, 13 * (l + 1))
                x3 = xx.rearrange("p (b h) -> p b h", b=2)
                step.then(tt(x3, ab[:, :, 0:6], pc("dtb", l, NH).unsqueeze(1).to_broadcast([P, 2, NH]), ALU.add))
                stt(l1, xx, -1.0, xx, ALU.mult, ALU.max).then_inc(gate_in, 1)
                dve.wait_ge(gate_ln, 2 * (l + 1))
                step.then(stt(xx, xx, 0.0, l1, ALU.max, ALU.add))
                na = nA[:, NH * l:NH * (l + 1)].unsqueeze(1).to_broadcast([P, 2, NH])
                step.then(tt(x3, x3, na, ALU.mult))
                v_.tensor_copy(by_bh(g_i), xx.rearrange("p (b j r) -> p b j r", b=2, j=3)).then_inc(g_ready, 1)
                dve.wait_ge(gate_tanh, l + 1)
                step(ts(beta, beta, 0.5, 0.5, ALU.mult, ALU.add))
                dve.wait_ge(y_psum, l + 1)
                for f in range(2):
                    stt_out = stt(ys[:, f, :], uT[:, f, :], par[:, PO["d"] + 2 * l + f:PO["d"] + 2 * l + f + 1],
                                  ps[:, 3, f * T:(f + 1) * T], ALU.mult, ALU.add)
                    if f:
                        stt_out.then_inc(y_sum, 1)
                    else:
                        step.then(stt_out)
                dve.wait_ge(g_ready, l + 1)
                tt(tg, C("cum").unsqueeze(1).to_broadcast([P, 12, P]), g_i.unsqueeze(2).to_broadcast([P, 12, P]),
                   ALU.mult).then_inc(tg_ready, 1)
                dve.wait_ge(glu_sig, 2 * (l + 1))
                step.then(stt(sig, sig, 1.0, ys, ALU.add, ALU.mult))
                ts(xT[:, 0:2, :], sig, 0.5, None, ALU.mult).then_inc(mix_ready, 1)
                dve.wait_ge(pv_psum, l + 1)
                step(v_.tensor_copy(xT[:, 2:4, :], ps[:, 1, :]))
                v_.tensor_copy(xT[:, 4, :], ps[:, 4, 0:T]).then_inc(pv_evac, 1)
                dve.wait_ge(gs_evac, l + 1)
                step(ts(ngc, gsum[:, 0:12], -1.0, None, ALU.mult))
                tt(ekl, gsum[:, 12:24], gsum[:, 0:12], ALU.subtract).then_inc(gs_dve, 1)
                dve.wait_ge(nrm_sqrt, 3 * (l + 1))
                step.then(v_.reciprocal(rn, rn))
                step(stt(qkv[:, 0:3, :], qkv[:, 0:3, :], SCALE, rn[:, 0:3, :], ALU.mult, ALU.mult))
                tt(qkv[:, 3:6, :], qkv[:, 3:6, :], rn[:, 3:6, :], ALU.mult).then_inc(qk_ready, 1)
                for q, bank in enumerate((7, 0, 1)):
                    dve.wait_ge(gb_psum, 3 * l + q + 1)
                    tt(dt_[:, 4 * q:4 * q + 4, :], ps[:, bank, :].rearrange("p (i c) -> p i c", i=4),
                       C("negu").unsqueeze(1).to_broadcast([P, 4, P]), ALU.add).then_inc(gb_evac, 1)
                dve.wait_ge(dt_exp, 12 * (l + 1))
                step.then(tt(dt_, dt_, beta.unsqueeze(2).to_broadcast([P, 12, P]), ALU.mult))
                for q, bank in enumerate((3, 6, 7, 0, 1, 4)):
                    dve.wait_ge(kk_psum, 6 * l + q + 1)
                    tt(LA[:, 2 * q:2 * q + 2], ps[:, bank, :].rearrange("p (i w c) -> p i w c", i=2, w=2),
                       dt_[:, 2 * q:2 * q + 2, :].unsqueeze(2).to_broadcast([P, 2, 2, P]), ALU.mult)\
                        .then_inc(la_ready, 1)
                idb = ident.unsqueeze(1)
                dve.wait_ge(m_ready, 6 * l + 1)
                tt(U, idb.to_broadcast([P, 12, P]), M[0], ALU.subtract).then_inc(u_ready, 1)
                for g in range(3):
                    dve.wait_ge(t_psum, 3 * l + g + 1)
                    tt(Tm[:, 4 * g:4 * g + 4, :], idb.to_broadcast([P, 4, P]),
                       ps[:, (0, 1, 3)[g], :].rearrange("p (i c) -> p i c", i=4), ALU.subtract).then_inc(t_ready, 1)
                dve.wait_ge(kv_evac, 3 * (l + 1))
                dve.wait_ge(gs_exp, 3 * (l + 1))
                step.wait()
                step.then(tt(ekl, ekl, beta, ALU.mult))
                for b in range(NB):
                    for dst, by in ((kg, eg), (kd, ekl)):
                        h4 = "p (j r d) -> p j r d"
                        step(tt(dst[:, b, :].rearrange(h4, j=3, r=2), kv[:, 0, b, :].rearrange(h4, j=3, r=2),
                                by_bh(by)[:, b].unsqueeze(3).to_broadcast([P, 3, 2, HD]), ALU.mult))
                step(tt(zt.rearrange("p b (h d) -> p (b h) d", h=NH), zt.rearrange("p b (h d) -> p (b h) d", h=NH),
                        pc("nw", l, HD).unsqueeze(1).to_broadcast([P, 12, HD]), ALU.mult))
                step.wait()
                v_.memset(S, 0.0).then_inc(s_zero, 1)
                for v in range(5):
                    for g in range(3):
                        n = 3 * v + g
                        i4 = slice(4 * g, 4 * g + 4)
                        dve.wait_ge(xy_psum, 15 * l + n + 1)
                        if v < 4:
                            step(tt(Tm[:, i4, :], Tm[:, i4, :], ps[:, (0, 1, 3)[g], :]
                                    .rearrange("p (i c) -> p i c", i=4), ALU.subtract))
                        step.wait()
                        tt(U[:, i4, :], U[:, i4, :], ps[:, (4, 6, 7)[g], :].rearrange("p (i c) -> p i c", i=4),
                           ALU.subtract).then_inc(xy_used, 1)
                for b in range(NB):
                    dve.wait_ge(up_psum_, NB * l + b + 1)
                    v_.tensor_copy(up[:, b, :], ps[:, (2, 5)[b], 0:384]).then_inc(up_evac, 1)
                for n in range(NC):
                    b, c = divmod(n, 2)
                    rows = slice(64 * c, 64 * c + 64)
                    dve.wait_ge(up_evac, NB * (l + 1))
                    dve.wait_ge(ws_psum, NC * l + n + 1)
                    tt(vp[rows, b, :], up[rows, b, :], ps[rows, 3, 0:384], ALU.subtract).then_inc(vp_ready, 1)
                    dve.wait_ge(qs_psum, NC * l + n + 1)
                    for r in range(2):
                        hr = slice(64 * r, 64 * r + 64)
                        by = eS.rearrange("p (c r j b) -> p c b r j", c=2, r=2, j=3)[hr, c, b, r]
                        step(tt(S[hr, :, hr], S[hr, :, hr], by.unsqueeze(2).to_broadcast([64, 3, HD]), ALU.mult))
                    tt(o[rows, b, :].rearrange("p (j r d) -> p j r d", j=3, r=2),
                       ps[rows, 4, 0:384].rearrange("p (j r d) -> p j r d", j=3, r=2),
                       by_bh(eg)[rows, b].unsqueeze(3).to_broadcast([64, 3, 2, HD]), ALU.mult).then_inc(qs_used, 1)
                    dve.wait_ge(su_psum, NC * l + n + 1)
                    step.wait()
                    for r in range(2):
                        hr = slice(64 * r, 64 * r + 64)
                        tt(S[hr, :, hr], S[hr, :, hr],
                           ps[hr, 6, 0:384].rearrange("p (j e) -> p j e", j=3)[:, :, hr], ALU.add)\
                            .then_inc(s_ready, 1)
                    if c:
                        dve.wait_ge(qs_used, NC * l + n + 1)
                        dve.wait_ge(av_psum, NB * l + b + 1)
                        tt(o[:, b, :], o[:, b, :], ps[:, 7, 0:384], ALU.add).then_inc(o_ready, 1)
                    dve.wait_ge(s_ready, 2 * (NC * l + n + 1))
                for b in range(NB):
                    o3 = o[:, b, :].rearrange("p (h d) -> p h d", h=NH)
                    dve.wait_ge(o_sq, NB * l + b + 1)
                    v_.tensor_reduce(ss[:, 6 * b:6 * b + 6], osq[:, b, :].rearrange("p (h d) -> p h d", h=NH),
                                     AX_X, ALU.add).then_inc(o_ss, 1)
                    dve.wait_ge(o_std, NB * l + b + 1)
                    step.then(v_.reciprocal(rsum[:, 6 * b:6 * b + 6], ss[:, 6 * b:6 * b + 6]))
                    step.then(tt(o3, o3, rsum[:, 6 * b:6 * b + 6].unsqueeze(2).to_broadcast([P, NH, HD]), ALU.mult))
                    tt(o[:, b, :], o[:, b, :], zt[:, b, :], ALU.mult).then_inc(og_ready, 1)
                for b in range(NB):
                    dve.wait_ge(ot_psum, NB * l + b + 1)
                    v_.tensor_copy(xT[:, 5:8, b * P:(b + 1) * P],
                                   ps[:, 3 + b, 0:384].rearrange("p (j t) -> p j t", j=3)).then_inc(mix_ready, 1)
                norm(2 * l, (0, 1, 2, 5), lambda b, c: dve.wait_ge(res_psum, 6 * l + 2 * b + c + 1))
                x_transposed(2 * l + 1, (4, 3, 6, 7))
                if l == 0:
                    for u in range(DENSE_UNITS):
                        dve.wait_ge(gate_silu, u + 1)
                        dve.wait_ge(up_psum, u + 1)
                        if u >= 2:
                            dve.wait_ge(ht_psum, u - 1)
                        tt(hh[u % 2], ps[:, 5, :], sg[u % 2], ALU.mult).then_inc(h_ready, 1)
                    norm(1, (0, 1, 2, 3), lambda b, c: dve.wait_ge((res_psum, down_done)[c],
                                                                  (4, DENSE_UNITS - NB)[c] + b + 1))

            def r8(a, n=16):
                return rt[:, a:a + n].rearrange("p (b e) -> p b e", b=2)

            lg, t8, oh1, oh2, sel_, l2 = (r8(16 * k) for k in range(6))
            m1, m2, ex, g1, g2 = (rt[:, 96 + 2 * k:98 + 2 * k] for k in (3, 4, 2, 5, 6))
            dif = rt[:, 98:100]
            rev = cst[:, C_REV:C_REV + NE].unsqueeze(1).to_broadcast([P, 2, NE])

            def b8(a):
                return a.unsqueeze(2).to_broadcast([P, 2, NE])

            dve.wait_ge(lg_psum, 1)
            step.then(v_.tensor_copy(lg, ps[:, 0, 0:16].rearrange("p (b e) -> p b e", b=2)))

            def first_max(src, m, one_hot):
                step.then(v_.tensor_reduce(m, src, AX_X, ALU.max))
                step.then(tt(t8, src, b8(m), ALU.is_equal))
                step.then(tt(t8, t8, rev, ALU.mult))
                step.then(v_.tensor_reduce(g1, t8, AX_X, ALU.max))
                step.then(tt(one_hot, rev, b8(g1), ALU.is_equal))

            first_max(lg, m1, oh1)
            step.then(stt(l2, oh1, NEG, lg, ALU.mult, ALU.add))
            first_max(l2, m2, oh2)
            tt(dif, m2, m1, ALU.subtract).then_inc(gate_exp_in, 1)
            tt(sel_, oh1, oh2, ALU.add).then_inc(sel_ready, 1)
            dve.wait_ge(gate_exp, 1)
            step.then(ts(g1, ex, 1.0, None, ALU.add))
            step.then(v_.reciprocal(g1, g1))
            step.then(tt(g2, ex, g1, ALU.mult))
            step(tt(oh1, oh1, b8(g1), ALU.mult))
            step.then(tt(oh2, oh2, b8(g2), ALU.mult))
            for e0 in (0, NE):
                step(tt(comb[:, :, e0:e0 + NE], oh1, oh2, ALU.add))
            step(v_.memset(comb[:, :, 16:17], 0.0))
            step(v_.memset(pos[:, :, 16:17], -1.0))
            dve.wait_ge(sel_ready, 1)
            dve.wait_ge(pos_psum, 1)
            step.then(stt(t8, ps[:, 1, 0:16].rearrange("p (b e) -> p b e", b=2), 1000.0, sel_, ALU.add, ALU.mult))
            step(ts(pos[:, :, 0:NE], t8, -1000.0, None, ALU.add))
            step(ts(pos[:, :, NE:2 * NE], t8, -1000.0 - P, None, ALU.add))
            step.then(v_.tensor_reduce(m1[:, 0:1], ps[:, 1, 16:24], AX_X, ALU.max))
            v_.tensor_copy(count_i[:, 0:1], m1[:, 0:1]).then_inc(route_ready, 1)
            for b in range(NB):
                ts(pick[:, b, :], C("iota"), pos[:, b, 0:1], None, ALU.is_equal).then_inc(pick_ready, 1)
            v_.memset(fa, 0.0).then_inc(sc_added, 1)
            dve.wait_ge(sc_added, 1)

            def gathered(n):
                dve.wait_ge(xg_psum, n)
                v_.tensor_copy(xg[:, 4:8, :], ps[:, 3, :]).then_inc(xg_dve, 1)

            gathered(2)

            def expert(i):
                u0 = i * FC + DENSE_UNITS
                for b in range(NB):
                    ts(pickw[:, b, :], C("iota"), pos[:, b, bass.ds(i, 1)], comb[:, b, bass.ds(i, 1)],
                       ALU.is_equal, ALU.mult).then_inc(pickw_ready, 1)
                dve.wait_ge(xg_psum, i * 2 + 2)
                for b in range(NB):
                    ts(pick[:, b, :], C("iota"), pos[:, b, bass.ds(i + 1, 1)], None, ALU.is_equal)\
                        .then_inc(pick_ready, 1)
                dve.wait_ge(pwt_psum, i + 1)
                v_.tensor_copy(pwT, ps[:, 7, 0:T]).then_inc(pwt_evac, 1)
                for j in range(FC):
                    dve.wait_ge(gate_silu, u0 + (j + 1))
                    dve.wait_ge(up_psum, u0 + (j + 1))
                    dve.wait_ge(ht_psum, u0 + max(j - 1, 0))
                    tt(hh[j % 2], ps[:, 5, :], sg[j % 2], ALU.mult).then_inc(h_ready, 1)
                dve.wait_ge(down_done, u0 + FC)
                v_.tensor_copy(ye[:, 512:1024], ps[:, 1, :]).then_inc(ye_dve, 1)
                gathered(i * 2 + 4)
                for k, bank in enumerate((7, 6, 2, 3)):
                    b, c = divmod(k, 2)
                    dve.wait_ge(sc_out, i * 4 + (k + 1))
                    f = fa[:, b, 512 * c:512 * (c + 1)]
                    tt(f, f, ps[:, bank, :], ALU.add).then_inc(sc_added, 1)
                dve.wait_ge(sc_added, i * 4 + 5)

            with dve.Fori(0, NE) as i:
                expert(i)
            most = dve.value_load(count_i[0:1, 0:1], min_val=0, max_val=T)
            with dve.If(most > P):
                with dve.Fori(NE, 2 * NE) as i:
                    expert(i)
            norm(3, None, None)

        @block.tensor
        def _(pe):
            mm, tr = nc.tensor.matmul, nc.tensor.transpose

            def chunk(m):
                pe.wait_ge(slot_loaded[m % SLOTS], 16 * (m // SLOTS + 1))

            def transpose_x(n, banks):
                for b in range(NB):
                    if n:
                        pe.wait_ge(x_ready, NB * (n - 1) + b + 1)
                    for k in range(KT):
                        c0 = (k % 2) * T + b * P
                        ins = tr(ps[:, banks[k // 2], c0:c0 + P], x[:, b, k * P:(k + 1) * P], ident)
                        if b and k % 2:
                            ins.then_inc(xt_psum, 1)
                pe.wait_ge(xt_act, 2 * (n + 1))
                pe.wait_ge(xt_dve, 2 * (n + 1))

            def features(bank, col, w, c0, last=None):
                for k in range(KT):
                    ins = mm(ps[:, bank, col:col + T], w[:, k, c0:c0 + P], xT[:, k, :], start=(k == 0),
                             stop=(k == KT - 1))
                return ins

            def tokens(bank, n, w, c0, b):
                for k in range(KT):
                    ins = mm(ps[:, bank, 0:n], xT[:, k, b * P:(b + 1) * P], w[:, k, c0:c0 + n], start=(k == 0),
                             stop=(k == KT - 1))
                return ins

            pe.wait_ge(cst_loaded, 16)
            pe.wait_ge(x_loaded, 32)
            for l in range(L):
                m0 = FIRST[l]
                transpose_x(2 * l, (0, 1, 6, 7))
                w = [slot_wide((m0 + c) % SLOTS, WIN[c][1]) for c in range(len(WIN))]
                chunk(m0)
                features(4, 0, w[0], 0)
                features(4, T, w[0], P).then_inc(proj_psum, 1)
                features(5, 0, w[0], 2 * P)
                features(5, T, w[0], 3 * P).then_inc(proj_psum, 1)
                chunk(m0 + 1)
                features(2, 0, w[1], 0)
                features(2, T, w[1], P).then_inc(proj_psum, 1)
                features(3, 0, w[1], 2 * P)
                features(3, T, w[1], 3 * P).then_inc(proj_psum, 1)

                def s5_in(t):
                    re, im = ((6, 0), (4, 2))[t]
                    for r, bank in ((0, re), (1, im)):
                        for jj in range(4):
                            ins = mm(ps[:, bank + jj // 2, (jj % 2) * T:(jj % 2 + 1) * T], b_pad[:, 4 * t + jj, r, :],
                                     uT[:, t, :], start=True, stop=True)
                    ins.then_inc(bu_psum, 1)

                pe.wait_ge(b_loaded, 16 * (l + 1))
                pe.wait_ge(proj_evac, 13 * l + 1)
                s5_in(0)
                chunk(m0 + 2)
                pe.wait_ge(proj_evac, 13 * l + 2)
                tokens(4, 384, w[2], 0, 0).then_inc(proj_psum, 1)
                tokens(5, 384, w[2], 0, 1).then_inc(proj_psum, 1)
                pe.wait_ge(proj_evac, 13 * l + 4)
                for h in range(NH):
                    bank = (2, 3, 6, 7, 0, 1)[h]
                    if h == 2:
                        pe.wait_ge(bu_used, 2 * l + 1)
                    j, rows = h // 2, slice(64 * (h % 2), 64 * (h % 2) + 64)
                    mm(ps[:, bank, 0:P], qkm[rows, j, 0:P], qkm[rows, 3 + j, 0:P], start=True, stop=True)
                    mm(ps[:, bank, P:3 * P], qkm[rows, j, P:T], qkm[rows, 3 + j, :], start=True, stop=True)\
                        .then_inc(sc_psum, 1)
                pe.wait_ge(proj_evac, 13 * l + 6)
                pe.wait_ge(sc_evac, NH * l + 2)
                s5_in(1)
                chunk(m0 + 3)
                pe.wait_ge(sc_evac, NH * l + 4)
                features(6, 0, w[3], 0)
                features(6, T, w[3], P).then_inc(proj_psum, 1)
                features(7, 0, w[3], 2 * P)
                features(7, T, w[3], 3 * P).then_inc(proj_psum, 1)
                chunk(m0 + 4)
                pe.wait_ge(sc_evac, NH * l + 6)
                features(0, 0, w[4], 0)
                features(0, T, w[4], P).then_inc(proj_psum, 1)
                features(1, 0, w[4], 2 * P)
                features(1, T, w[4], 3 * P).then_inc(proj_psum, 1)
                chunk(m0 + 5)
                pe.wait_ge(bu_used, 2 * l + 2)
                features(4, 0, w[5], 0).then_inc(proj_psum, 1)
                tokens(5, ZAB, w[5], P, 0).then_inc(proj_psum, 1)
                tokens(2, ZAB, w[5], P, 1).then_inc(proj_psum, 1)
                pe.wait_ge(c_ready, l + 1)
                pe.wait_ge(states_ready, 2 * (l + 1))
                for f in range(2):
                    for k in range(8):
                        j, r = 4 * f + k // 2, k % 2
                        ins = mm(ps[:, 3, f * T:(f + 1) * T], c_pad[:, j, r, :], states[r][:, j, :],
                                 start=(k == 0), stop=(k == 7))
                ins.then_inc(y_psum, 1)
                pe.wait_ge(glu_loaded, 16 * (l + 1))
                pe.wait_ge(y_gelu, l + 1)
                pe.wait_ge(proj_evac, 13 * l + 7)
                for f in range(2):
                    for k in range(2):
                        ins = mm(ps[:, 6, f * T:(f + 1) * T], gw[:, k, f * P:(f + 1) * P], ys[:, k, :],
                                 start=(k == 0), stop=(k == 1))
                ins.then_inc(glu_psum, 1)
                pe.wait_ge(sc_norm, 2 * (l + 1))
                pe.wait_ge(proj_evac, 13 * l + 9)
                for h in range(NH):
                    if h >= 2:
                        pe.wait_ge(pt_evac, NH * l + h - 1)
                    for q in range(3):
                        ins = tr(ps[:, (7, 0)[h % 2], q * P:(q + 1) * P], sc[:, h, q * P:(q + 1) * P], ident)
                    ins.then_inc(pt_psum, 1)
                pe.wait_ge(pt_evac, NH * (l + 1))
                pe.wait_ge(proj_evac, 13 * l + 11)
                for h in range(NH):
                    j, rows = h // 2, slice(64 * (h % 2), 64 * (h % 2) + 64)
                    bank, c0 = ((1, 0), (1, T), (4, 0))[j]
                    vc = slice(h * HD, (h + 1) * HD)
                    mm(ps[rows, bank, c0:c0 + P], mv[:, 0, vc], pT[:, h, 0:P], start=True, stop=True)
                    mm(ps[rows, bank, c0 + P:c0 + T], mv[:, 0, vc], pT[:, h, P:2 * P], start=True, stop=False)
                    ins = mm(ps[rows, bank, c0 + P:c0 + T], mv[:, 1, vc], pT[:, h, 2 * P:3 * P], start=False,
                             stop=True)
                ins.then_inc(pv_psum, 1)
                pe.wait_ge(g_ready, l + 1)
                pe.wait_ge(proj_evac, 13 * (l + 1))
                for q, name in enumerate(("cum", "same", "ch0", "ch1")):
                    ins = mm(ps[:, 5, 12 * q:12 * q + 12], C(name), g_i, start=True, stop=True)
                ins.then_inc(gs_psum, 1)
                pe.wait_ge(sq_done, l + 1)
                pe.wait_ge(glu_sig, 2 * (l + 1))
                for q, bank in enumerate((2, 3, 6)):
                    mm(ps[:, bank, :], C("same"), sq[:, 2 * q:2 * q + 2, :], start=True, stop=True)\
                        .then_inc(nrm_psum, 1)
                pe.wait_ge(tg_ready, l + 1)
                pe.wait_ge(pv_evac, l + 1)
                for q, bank in enumerate((7, 0, 1)):
                    mm(ps[:, bank, :], C("ones"), tg[:, 4 * q:4 * q + 4, :], start=True, stop=True)\
                        .then_inc(gb_psum, 1)
                pe.wait_ge(qk_ready, l + 1)
                pe.wait_ge(silu_done, 3 * (l + 1))
                pe.wait_ge(gs_evac, l + 1)
                pe.wait_ge(nrm_sqrt, 3 * (l + 1))
                for n in range(12):
                    wh, b, j = n // 6, (n // 3) % 2, n % 3
                    ins = tr(ps[:, (4, 5, 2)[n // 4], (n % 4) * P:(n % 4 + 1) * P],
                             qkv[:, 3 + 3 * wh + j, b * P:(b + 1) * P], ident)
                    if n % 4 == 3:
                        ins.then_inc(kv_psum, 1)
                pe.wait_ge(gb_evac, 3 * (l + 1))
                pe.wait_ge(kv_evac, 3 * l + 1)
                for jb in range(6):
                    for r in range(2):
                        i = 6 * r + jb
                        j, b = jb // 2, jb % 2
                        rows = slice(64 * r, 64 * r + 64)
                        bank = (3, 6, 7, 0, 1, 4)[i // 2]
                        c0 = (i % 2) * T
                        ins = mm(ps[:, bank, c0:c0 + T].rearrange("p (w c) -> p w c", w=2),
                                 qkv[rows, 3 + j, b * P:(b + 1) * P], qkv[rows, j:j + 4:3, b * P:(b + 1) * P],
                                 start=True, stop=True)
                ins.then_inc(kk_psum, 6)
                pe.wait_ge(m_ready, 6 * l + 1)
                pe.wait_ge(la_ready, 6 * (l + 1))
                for g in range(3):
                    for i in range(4):
                        ins = tr(ps[:, (0, 1, 3)[g], i * P:(i + 1) * P], M[0][:, 4 * g + i, :], ident)
                    ins.then_inc(t_psum, 1)
                pe.wait_ge(u_ready, l + 1)
                pe.wait_ge(kv_evac, 3 * (l + 1))
                for v in range(5):
                    pe.wait_ge(m_ready, 6 * l + v + 2)
                    for g in range(3):
                        n = 3 * v + g
                        if v == 0:
                            pe.wait_ge(t_ready, 3 * l + g + 1)
                        else:
                            pe.wait_ge(xy_used, 15 * l + n - 2)
                        if n >= 2:
                            pe.wait_ge(a_evac, 15 * l + n - 1)
                        for i in range(4 * g, 4 * g + 4):
                            ins = mm(ps[:, (2, 5)[n % 2], (i % 4) * P:(i % 4 + 1) * P], M[(v + 1) % 2][:, i, :],
                                     Tm[:, i, :], start=True, stop=True)
                        ins.then_inc(a_psum, 1)
                    for g in range(3):
                        n = 3 * v + g
                        pe.wait_ge(a_evac, 15 * l + n + 1)
                        for i in range(4 * g, 4 * g + 4):
                            c0 = (i % 4) * P
                            if v < 4:
                                mm(ps[:, (0, 1, 3)[g], c0:c0 + P], U[:, i, :], A[:, i, :], start=True, stop=True)
                            ins = mm(ps[:, (4, 6, 7)[g], c0:c0 + P], A[:, i, :], U[:, i, :], start=True, stop=True)
                        ins.then_inc(xy_psum, 1)
                pe.wait_ge(xy_used, 15 * (l + 1))
                pe.wait_ge(a_evac, 15 * (l + 1))
                pe.wait_ge(s_zero, l + 1)
                for j in range(3):
                    for b in range(NB):
                        for r in range(2):
                            i = 6 * r + 2 * j + b
                            ins = mm(ps[64 * r:64 * r + 64, j // 2, (j % 2) * T + b * P:(j % 2) * T + (b + 1) * P],
                                     kg[:, b, (2 * j + r) * HD:(2 * j + r + 1) * HD], U[:, i, :],
                                     start=True, stop=True)
                ins.then_inc(w_psum, 2)
                for b in range(NB):
                    for h in range(NH):
                        i = 6 * (h % 2) + 2 * (h // 2) + b
                        ins = mm(ps[:, (2, 5)[b], h * HD:(h + 1) * HD], U[:, i, :],
                                 kv[:, 1, b, h * HD:(h + 1) * HD], start=True, stop=True)
                    ins.then_inc(up_psum_, 1)
                pe.wait_ge(w_evac, 2 * (l + 1))
                wo = [slot_tall((m0 + 6 + c) % SLOTS) for c in range(2)]

                def project(k, bank_at, first, final):
                    b, c = divmod(bank_at, 2)
                    return mm(ps[:, (0, 1, 2, 5)[bank_at], :], xT[:, k, b * P:(b + 1) * P],
                              wo[k // 4][:, k % 4, 512 * c:512 * (c + 1)], start=first, stop=final)

                for n in range(NC):
                    b, c = divmod(n, 2)
                    rows = slice(64 * c, 64 * c + 64)
                    toks = slice(n * CH, (n + 1) * CH)
                    if n:
                        pe.wait_ge(s_ready, 2 * (NC * l + n))
                    for j in range(3):
                        ins = mm(ps[rows, 3, j * P:(j + 1) * P], wT[:, j, toks], S[:, j, :], start=True, stop=True)
                    ins.then_inc(ws_psum, 1)
                    if n:
                        pe.wait_ge(qs_used, NC * l + n)
                    for j in range(3):
                        ins = mm(ps[rows, 4, j * P:(j + 1) * P], qkv[:, j, toks], S[:, j, :], start=True, stop=True)
                    ins.then_inc(qs_psum, 1)
                    pe.wait_ge(vp_ready, NC * l + n + 1)
                    for j in range(3):
                        ins = mm(ps[:, 6, j * P:(j + 1) * P], kd[rows, b, j * P:(j + 1) * P],
                                 vp[rows, b, j * P:(j + 1) * P], start=True, stop=True)
                    ins.then_inc(su_psum, 1)
                    if c:
                        if b:
                            pe.wait_ge(o_ready, NB * l + 1)
                        for h in range(NH):
                            i = 6 * (h % 2) + 2 * (h // 2) + b
                            ins = mm(ps[:, 7, h * HD:(h + 1) * HD], LA[:, i, 0, :], vp[:, b, h * HD:(h + 1) * HD],
                                     start=True, stop=True)
                        ins.then_inc(av_psum, 1)
                    if n == 0:
                        chunk(m0 + 6)
                        chunk(m0 + 7)
                        pe.wait_ge(up_evac, NB * (l + 1))
                        pe.wait_ge(mix_ready, 3 * l + 1)
                    for k in ((0, 1), (2,), (3,), (4,))[n]:
                        for q in range(4):
                            ins = project(k, q, k == 0, False)
                        if k == 3:
                            ins.then_inc(wo_used, 1)
                for b in range(NB):
                    pe.wait_ge(og_ready, NB * l + b + 1)
                    for j in range(3):
                        ins = tr(ps[:, 3 + b, j * P:(j + 1) * P], o[:, b, j * P:(j + 1) * P], ident)
                    ins.then_inc(ot_psum, 1)
                for b in range(NB):
                    pe.wait_ge(mix_ready, 3 * l + 2 + b)
                    for c in range(2):
                        for k in range(5, 8):
                            ins = project(k, 2 * b + c, False, k == 7)
                        ins.then_inc(res_psum, 1)
                transpose_x(2 * l + 1, (4, 3, 6, 7))

                if l == 0:
                    def hidden_T(u):
                        pe.wait_ge(h_ready, u + 1)
                        if u >= 2:
                            pe.wait_ge(ht_evac, u - 1)
                        for q in range(4):
                            ins = tr(ps[:, 6 + u % 2, q * P:(q + 1) * P], hh[u % 2][:, q * P:(q + 1) * P], ident)
                        ins.then_inc(ht_psum, 1)

                    def down(u):
                        j, b = divmod(u, NB)
                        m = PER_LAYER + 3 * j + 2
                        chunk(m)
                        pe.wait_ge(ht_evac, u + 1)
                        for c in range(2):
                            for q in range(4):
                                ins = mm(ps[:, 2 * b + c, :], hT[u % 2][:, q, :],
                                         slot_tall(m % SLOTS)[:, q, 512 * c:512 * (c + 1)],
                                         start=(j == 0 and q == 0), stop=(j == FC - 1 and q == 3))
                            if j == FC - 1 and c == 0:
                                ins.then_inc(res_psum, 1)
                        ins.then_inc(down_done, 1)

                    for u in range(DENSE_UNITS):
                        j, b = divmod(u, NB)
                        m = PER_LAYER + 3 * j
                        for w_, bank, s_psum in ((0, 4, gate_psum), (1, 5, up_psum)):
                            chunk(m + w_)
                            if u:
                                pe.wait_ge((gate_silu, h_ready)[w_], u)
                            wv = slot_wide((m + w_) % SLOTS)
                            for k in range(KT):
                                ins = mm(ps[:, bank, :], xT[:, k, b * P:(b + 1) * P], wv[:, k, :],
                                         start=(k == 0), stop=(k == KT - 1))
                            ins.then_inc(s_psum, 1)
                            if u and w_ == 0:
                                hidden_T(u - 1)
                        if u:
                            down(u - 1)
                    hidden_T(DENSE_UNITS - 1)
                    down(DENSE_UNITS - 1)

            rw = par[:, PO["router"]:PO["router"] + KT * NE].rearrange("p (k e) -> p k e", k=KT)
            for b in range(NB):
                for k in range(KT):
                    ins = mm(ps[:, 0, NE * b:NE * (b + 1)], xT[:, k, b * P:(b + 1) * P], rw[:, k, :],
                             start=(k == 0), stop=(k == KT - 1))
            ins.then_inc(lg_psum, 1)
            pe.wait_ge(sel_ready, 1)
            sel_ = rt[:, 64:80]
            mm(ps[:, 1, 0:8], C("before"), sel_[:, 0:8], start=True, stop=True)
            mm(ps[:, 1, 8:16], C("ones"), sel_[:, 0:8], start=True, stop=False)
            mm(ps[:, 1, 8:16], C("before"), sel_[:, 8:16], start=False, stop=True)
            mm(ps[:, 1, 16:24], C("ones"), sel_[:, 0:8], start=True, stop=False)
            mm(ps[:, 1, 16:24], C("ones"), sel_[:, 8:16], start=False, stop=True).then_inc(pos_psum, 1)

            def gather(half):
                for k in range(4 * half, 4 * half + 4):
                    for b in range(NB):
                        ins = mm(ps[:, 2 + half, (k % 4) * P:(k % 4 + 1) * P], x[:, b, k * P:(k + 1) * P],
                                 pick[:, b, :], start=(b == 0), stop=(b == NB - 1))
                ins.then_inc(xg_psum, 1)

            pe.wait_ge(pick_ready, 2)
            gather(0)
            gather(1)
            pre = [len([m for m in range(N_PRE) if m % SLOTS == s]) if s < SLOTS else 0 for s in range(NSLOT)]

            def expert(i):
                u0 = i * FC + DENSE_UNITS

                def loaded(r):
                    s = r % NSLOT
                    pe.wait_ge(slot_loaded[s], i * (16 * EXP // NSLOT) + 16 * (pre[s] + r // NSLOT + 1))

                def hidden_T(j):
                    pe.wait_ge(h_ready, u0 + (j + 1))
                    pe.wait_ge(ht_evac, u0 + max(j - 1, 0))
                    for q in range(4):
                        ins = tr(ps[:, 6 + j % 2, q * P:(q + 1) * P], hh[j % 2][:, q * P:(q + 1) * P], ident)
                    ins.then_inc(ht_psum, 1)

                def down(j):
                    r = 3 * j + 2
                    loaded(r)
                    pe.wait_ge(ht_evac, u0 + (j + 1))
                    for c in range(2):
                        for q in range(4):
                            ins = mm(ps[:, c, :], hT[j % 2][:, q, :], slot_tall(r % NSLOT)[:, q, 512 * c:512 * (c + 1)],
                                     start=(j == 0 and q == 0), stop=(j == FC - 1 and q == 3))
                    ins.then_inc(down_done, 1)

                for j in range(FC):
                    for w_, bank, s_psum in ((0, 4, gate_psum), (1, 5, up_psum)):
                        r = 3 * j + w_
                        loaded(r)
                        pe.wait_ge((gate_silu, h_ready)[w_], u0 + j)
                        if j == 0 and w_ == 0:
                            pe.wait_ge(xg_act, i + 1)
                            pe.wait_ge(xg_dve, i + 1)
                        wv = slot_wide(r % NSLOT)
                        for k in range(KT):
                            ins = mm(ps[:, bank, :], xg[:, k, :], wv[:, k, :], start=(k == 0), stop=(k == KT - 1))
                        ins.then_inc(s_psum, 1)
                        if not (j or w_):
                            pe.wait_ge(pickw_ready, i * 2 + 2)
                            pe.wait_ge(sc_added, i * 4 + 1)
                            for b in range(NB):
                                t_ = tr(ps[:, 7, b * P:(b + 1) * P], pickw[:, b, :], ident)
                            t_.then_inc(pwt_psum, 1)
                        if j and w_ == 0:
                            if j == 2:
                                pe.wait_ge(pwt_evac, i + 1)
                            hidden_T(j - 1)
                    if j:
                        down(j - 1)
                pe.wait_ge(pick_ready, i * 2 + 4)
                gather(0)
                hidden_T(FC - 1)
                down(FC - 1)
                gather(1)
                pe.wait_ge(ye_act, i + 1)
                pe.wait_ge(ye_dve, i + 1)
                pe.wait_ge(pwt_evac, i + 1)
                pe.wait_ge(ht_evac, u0 + FC)
                for k, bank in enumerate((7, 6, 2, 3)):
                    if k == 2:
                        pe.wait_ge(xg_act, i + 2)
                        pe.wait_ge(xg_dve, i + 2)
                    b, c = divmod(k, 2)
                    mm(ps[:, bank, :], pwT[:, b * P:(b + 1) * P], ye[:, 512 * c:512 * (c + 1)], start=True,
                       stop=True).then_inc(sc_out, 1)

            with pe.Fori(0, NE) as i:
                expert(i)
            pe.wait_ge(route_ready, 1)
            most = pe.value_load(count_i[0:1, 0:1], min_val=0, max_val=T)
            with pe.If(most > P):
                with pe.Fori(NE, 2 * NE) as i:
                    expert(i)


def tiles(a):
    return np.moveaxis(a.reshape(*a.shape[:-1], a.shape[-1] // P, P), -1, 0)


def kernel(x, w_in, w_out, s5_lam_re, s5_lam_im, s5_log_dt, s5_b_re, s5_b_im, s5_c_re, s5_c_im, s5_d, s5_glu_w,
           s5_glu_b, gdn_conv_w, gdn_a_log, gdn_dt_bias, gdn_norm_w, ln1_g, ln1_b, ln2_g, ln2_b, ffn_w_gate,
           ffn_w_up, ffn_w_down, moe_router, moe_w_gate, moe_w_up, moe_w_down):
    import concourse.bacc as bacc
    from concourse.bass_utils import run_bass_kernel_spmd

    f32 = np.float32
    arr = {k: np.asarray(v) for k, v in dict(
        x_in=x, w_in=w_in, w_out=w_out, wg=ffn_w_gate, wu=ffn_w_up, wd=ffn_w_down, mg=moe_w_gate, mu=moe_w_up,
        md=moe_w_down).items()}
    G, N, Q = 16, 64, 16
    by_state = lambda a: np.asarray(a).reshape(L, ST, P).transpose(2, 0, 1).reshape(P, L * ST)
    c_lay = np.zeros((P, L, ST, 2, 16), f32)
    b_lay = np.zeros((L, P, ST, 2, P), f32)
    for r, (bb, cc) in enumerate(((np.asarray(s5_b_re), np.asarray(s5_c_re)), (np.asarray(s5_b_im), np.asarray(s5_c_im)))):
        for g in range(G):
            j, half = divmod(g, 2)
            c_lay[64 * half:64 * half + 64, :, j, r, :] = cc[:, g].transpose(2, 0, 1)
            f0 = 16 * (g % 8)
            b_lay[:, f0:f0 + 16, j, r, 64 * half:64 * half + 64] = bb[:, g].transpose(0, 2, 1)
    rows = lambda a: np.broadcast_to(np.asarray(a).reshape(1, -1), (P, np.asarray(a).size))
    par = np.zeros((P, PW), f32)
    for name, v in (("lre", by_state(s5_lam_re)), ("lim", by_state(s5_lam_im)),
                    ("ldt", by_state(np.broadcast_to(np.asarray(s5_log_dt)[:, :, None], (L, G, N)))),
                    ("d", tiles(np.asarray(s5_d).reshape(L, S5W)).reshape(P, -1)),
                    ("gb", tiles(np.asarray(s5_glu_b)).reshape(P, -1)),
                    ("conv", tiles(np.asarray(gdn_conv_w)).transpose(0, 1, 3, 2).reshape(P, -1)),
                    ("alog", rows(gdn_a_log)), ("dtb", rows(gdn_dt_bias)), ("nw", rows(gdn_norm_w)),
                    ("c", c_lay.reshape(P, -1)),
                    ("router", np.asarray(moe_router)[0].reshape(KT, P, NE).transpose(1, 0, 2).reshape(P, -1))):
        par[:, PO[name]:PO[name] + v.shape[1]] = v
    arr["consts"] = constant_table()
    arr["params"] = par
    arr["s5_b"] = b_lay.reshape(L, P, ST * 2 * P)
    arr["glu_w"] = np.asarray(s5_glu_w).reshape(L, 2, P, S5W).transpose(0, 2, 1, 3).reshape(L, P, 512)
    arr["ln"] = np.stack([np.stack([np.asarray(g)[l], np.asarray(b)[l]]) for l in range(L)
                          for g, b in ((ln1_g, ln1_b), (ln2_g, ln2_b))])
    nc = bacc.Bacc("TRN2", target_bir_lowering=False, num_devices=1)
    order = ("x_in", "w_in", "w_out", "consts", "params", "s5_b", "glu_w", "ln", "wg", "wu", "wd", "mg", "mu", "md")
    sent, args = {}, []
    for name in order:
        a = np.ascontiguousarray(arr[name])
        sent[f"in_{name}"] = a
        args.append(nc.dram_tensor(f"in_{name}", a.shape, mybir.dt.from_np(a.dtype), kind="ExternalInput").ap())
    out = nc.dram_tensor("out_0", (1, T, D), F32, kind="ExternalOutput").ap()
    build(nc, *args, out)
    r = run_bass_kernel_spmd(nc, [sent], core_ids=[0])
    return r.results[0]["out_0"]
```

```python
from contextlib import ExitStack

import numpy as np
import concourse.bass as bass
from concourse import mybir

ALU = mybir.AluOpType
ACT = mybir.ActivationFunctionType
F32 = mybir.dt.float32
F32R = mybir.dt.float32r
I32 = mybir.dt.int32
AX_X = mybir.AxisListType.X

P = 128
D = 1024
T = 256
L = 2
NB = T // P
KT = D // P
S5W, MBW, GDW = 256, 384, 384
HD = 64
NH = 6
CH = 64
NC = T // CH
ST = 8
FF = 3584
FC = FF // 512
NE = 8
ALPHA = float((2 * L) ** 0.25)
SCALE = HD ** -0.5
NEG = -1.0e30

C_U, C_Q, C_K, C_V = 0, 256, 640, 1024
C_G, C_Z = 1408, 2560
IN_COLS = 2956
ZAB = IN_COLS - C_Z
WIN = [(0, 512), (512, 512), (1024, 384), (1408, 512), (1920, 512), (2432, 524)]
SLOT = KT * 524
SLOTS = 4

PIECE = 2048
RAWS, PARTS = 7, 3
SEQ = [(w, 0, p) for w in "GU" for p in range(2)]
for _j in range(1, FC):
    SEQ += [(w, _j, p) for w in "GU" for p in range(2)] + [("D", _j - 1, p) for p in range(2)]
SEQ += [("D", FC - 1, p) for p in range(2)]
AT = {key: r for r, key in enumerate(SEQ)}
NP = len(SEQ)
assert NP % RAWS == 0 and NP % PARTS == 0

_names = ["ident", "cum", "same", "ch0", "ch1", "ones", "causal", "negu", "lv0", "lv1", "lv2", "lv3", "lv4", "lv5",
          "before", "iota"]
CO = {n: 128 * i for i, n in enumerate(_names)}
C_REV = 128 * len(_names)
C_EPS6, C_EPS5, C_HPI, C_ONE = C_REV + 8, C_REV + 9, C_REV + 10, C_REV + 11
CW = C_REV + 12


def constant_table():
    r = np.arange(P)
    a, b = r[:, None], r[None, :]
    same = (a // CH) == (b // CH)
    c = np.zeros((P, CW), np.float32)

    def put(name, v):
        c[:, CO[name]:CO[name] + P] = v

    put("ident", a == b)
    put("cum", (a <= b) & same)
    put("same", same)
    put("ch0", a < CH)
    put("ch1", a >= CH)
    put("ones", 1.0)
    put("causal", np.where(b <= a, 0.0, NEG))
    put("negu", np.where((a <= b) & same, 0.0, NEG))
    for v in range(6):
        s = 1 << v
        put(f"lv{v}", ((b // s) % 2 == 1) & (a // s == b // s - 1))
    put("before", a < b)
    put("iota", np.broadcast_to(b, (P, P)))
    c[:, C_REV:C_REV + NE] = NE - np.arange(NE)
    c[:, C_EPS6], c[:, C_EPS5], c[:, C_HPI], c[:, C_ONE] = 1e-6, 1e-5, np.pi / 2, 1.0
    return c


PO, PW = {}, 0
for _n, _w in (("lre", L * ST), ("lim", L * ST), ("ldt", L * ST), ("d", L * 2), ("gb", L * 2), ("conv", L * 36),
               ("alog", L * NH), ("dtb", L * NH), ("nw", L * HD), ("c", L * ST * 32), ("router", KT * NE)):
    PO[_n] = PW
    PW += _w

A_XT, A_SLOTS = 0, KT * T
A_ZS = A_SLOTS + SLOTS * SLOT
A_ZF = A_ZS + 12544
A_PHASE = A_ZF + 9248
ARENA = A_PHASE + 2 * ST * T
A_RAW = A_SLOTS
A_XS = A_RAW + RAWS * PIECE
A_HI = A_XS + 2 * D * NB
A_LO = A_HI + PARTS * PIECE
A_HT = A_LO + PARTS * PIECE
A_SG = A_HT + 4096
A_H = A_SG + 1024
A_PK = A_H + 1024
assert A_H + 1024 <= A_PHASE
O_BP, O_CP, O_M, O_S = 0, 2304, 4352, 8448
O_PT = 0
O_DT, O_U, O_T, O_A, O_MM, O_LA = 0, 1536, 3072, 4608, 6144, 9216
O_SQ, O_RN, O_TG = 4608, 6144, 7680
O_SIG = 12032
O_QKV, O_Z = 0, 2304
O_UT, O_QKM, O_MV, O_CIN, O_Y, O_GW = 3072, 3584, 5120, 5888, 8224, 8736
O_KV, O_KG, O_KD, O_UP, O_WT, O_VP, O_O, O_ST = 3072, 4608, 5376, 6144, 6912, 7680, 8448, 3072

def build(nc, x_in, w_in, w_out, consts, params, s5_b, glu_w, ln, wg, wu, wd, mg, mu, md, out):
    ctx = ExitStack()
    with ctx:
        def sb(name, cols, dt=F32):
            return ctx.enter_context(nc.sbuf_tensor(name, [P, cols], dt))

        sems = {}

        def sem(name):
            sems[name] = ctx.enter_context(nc.semaphore(name))
            return sems[name]

        arena = sb("arena", ARENA)
        arena_at = nc.sbuf_base - 4 * ARENA

        def parts(name, at, cols):
            return nc.alloc_sbuf_tensor_at(name, [P, cols], F32R, offset=arena_at + 4 * at)

        x = sb("x", NB * D)[:, :].rearrange("p (b d) -> p b d", b=NB)
        xT = arena[:, A_XT:A_XT + KT * T].rearrange("p (k t) -> p k t", k=KT)
        cst = sb("cst", CW)
        par = sb("par", PW)
        score_rows = sb("score_rows", NH * 3 * P)
        lnrow = score_rows[:, 0:2 * D].rearrange("p (g d) -> p g d", g=2)
        phase = arena[:, A_PHASE:A_PHASE + 2 * ST * T]
        s5s = sb("s5s", 24 * L * ST)
        small = sb("small", 256)
        count_i = sb("count_i", 2, I32)
        pos = sb("pos", 2 * 17)[:, :].rearrange("p (b e) -> p b e", b=2)
        comb = sb("comb", 2 * 17)[:, :].rearrange("p (b e) -> p b e", b=2)
        rt = sb("rt", 160)
        ps = ctx.enter_context(nc.psum_tensor("ps", [P, 8, 512], F32))

        def C(name, rows=slice(0, P)):
            return cst[rows, CO[name]:CO[name] + P]

        ident = C("ident")

        def slot(s):
            return arena[:, A_SLOTS + s * SLOT:A_SLOTS + (s + 1) * SLOT]

        def zs(o, n):
            return arena[:, A_ZS + o:A_ZS + o + n]

        def zf(o, n):
            return arena[:, A_ZF + o:A_ZF + o + n]

        cos_t = phase[:, 0:ST * T].rearrange("p (j t) -> p j t", j=ST)
        sin_t = phase[:, ST * T:2 * ST * T].rearrange("p (j t) -> p j t", j=ST)
        b_pad = zs(O_BP, 2048).rearrange("p (j r s) -> p j r s", j=ST, r=2)
        c_pad = zs(O_CP, 2048).rearrange("p (j r f) -> p j r f", j=ST, r=2)
        mt = [zs(O_M + 1024 * i, 1024) for i in range(4)]
        states = [zs(O_S + 2048 * r, 2048).rearrange("p (j t) -> p j t", j=ST) for r in range(2)]
        uT = zf(O_UT, 512).rearrange("p (f t) -> p f t", f=2)
        gw = zf(O_GW, 512).rearrange("p (k n) -> p k n", k=2)
        ys = zf(O_Y, 512).rearrange("p (f t) -> p f t", f=2)
        sig = zs(O_SIG, 512).rearrange("p (f t) -> p f t", f=2)
        qkm = zf(O_QKM, 1536).rearrange("p (t n) -> p t n", t=6)
        mv = zf(O_MV, 768).rearrange("p (b n) -> p b n", b=2)
        sc = score_rows[:, :].rearrange("p (h n) -> p h n", h=NH)
        pT = zs(O_PT, 2304).rearrange("p (h n) -> p h n", h=NH)
        qkv = zf(O_QKV, 2304).rearrange("p (c t) -> p c t", c=9)
        zt = zf(O_Z, 768).rearrange("p (b n) -> p b n", b=2)
        cin = zf(O_CIN, 9 * 259).rearrange("p (c t) -> p c t", c=9)
        sq = zs(O_SQ, 1536).rearrange("p (c t) -> p c t", c=6)
        rn = zs(O_RN, 1536).rearrange("p (c t) -> p c t", c=6)

        def by_pair(o):
            return zs(o, 1536).rearrange("p (i c) -> p i c", i=12)

        tg, dt_, U, Tm, A = by_pair(O_TG), by_pair(O_DT), by_pair(O_U), by_pair(O_T), by_pair(O_A)
        M = [by_pair(O_MM), by_pair(O_MM + 1536)]
        LA = zs(O_LA, 3072).rearrange("p (i w c) -> p i w c", i=12, w=2)
        kv = zf(O_KV, 1536).rearrange("p (w b n) -> p w b n", w=2, b=2)
        kg = zf(O_KG, 768).rearrange("p (b n) -> p b n", b=2)
        kd = zf(O_KD, 768).rearrange("p (b n) -> p b n", b=2)
        up = zf(O_UP, 768).rearrange("p (b n) -> p b n", b=2)
        wT = zf(O_WT, 768).rearrange("p (j t) -> p j t", j=3)
        vp = zf(O_VP, 768).rearrange("p (b n) -> p b n", b=2)
        o = zf(O_O, 768).rearrange("p (b n) -> p b n", b=2)
        S = zf(O_ST, 384).rearrange("p (j e) -> p j e", j=3)
        osq = up
        raw = [arena[:, A_RAW + PIECE * i:A_RAW + PIECE * (i + 1)] for i in range(RAWS)]
        hi = [parts(f"hi{i}", A_HI + PIECE * i, PIECE) for i in range(PARTS)]
        lo = [parts(f"lo{i}", A_LO + PIECE * i, PIECE) for i in range(PARTS)]
        xs = [parts(f"xs{i}", A_XS + NB * D * i, NB * D) for i in range(2)]
        xs_x = [t[:, :].rearrange("p (k t) -> p k t", k=KT) for t in xs]
        hT_d = [[parts(f"hTd{i}{q}", A_HT + 2048 * i + 1024 * q, 1024) for q in range(2)] for i in range(2)]
        hT_e = [[parts(f"hTe{i}{q}", A_HT + 1024 * i + 512 * q, 512) for q in range(2)] for i in range(2)]
        ye = [parts(f"ye{q}", A_HT + 2048 + 1024 * q, 1024) for q in range(2)]
        xg = [parts(f"xg{q}", A_XT + D * q, D) for q in range(2)]
        sg = arena[:, A_SG:A_SG + 1024]
        hh = arena[:, A_H:A_H + 1024]
        pick = parts("pick", A_PK, T)[:, :].rearrange("p (b s) -> p b s", b=2)
        pickT = parts("pickT", A_PK + T, T)

        def sm(a, n):
            return small[:, a:a + n]

        ab = sm(0, 24).rearrange("p (b c) -> p b c", b=2)
        xx, l1, beta, g_i, gsum = sm(24, 12), sm(36, 12), sm(48, 12), sm(60, 12), sm(72, 48)
        eg, ekl, eS, ngc, rsum, rinv = sm(120, 12), sm(132, 12), sm(144, 24), sm(168, 12), sm(180, 12), sm(192, 12)
        nmax, ss = sm(204, 12), sm(216, 12)
        stats, mvar, rstd = sm(228, 12), sm(240, 2), sm(242, 1)
        nA = sm(244, 12)
        std = sb("std", 4)
        ctmp = sb("ctmp", T)[:, :]
        gbh = sb("gbh", 4)

        def by_bh(t):
            return t.rearrange("p (r j b) -> p b j r", r=2, j=3)

        slot_loaded = [sem(f"slot_loaded_{s}") for s in range(SLOTS)]
        raw_loaded = [sem(f"raw_loaded_{s}") for s in range(RAWS)]
        hi_ready, lo_ready, piece_used = sem("hi_ready"), sem("lo_ready"), sem("piece_used")
        wo_used = sem("wo_used")
        x_loaded, cst_loaded, par_loaded, b_loaded, glu_loaded, ln_loaded = (
            sem(n) for n in ("x_loaded", "cst_loaded", "par_loaded", "b_loaded", "glu_loaded", "ln_loaded"))
        ident_loaded, tail_loaded = sem("ident_loaded"), sem("tail_loaded")
        x_ready, xt_psum, xt_act, xt_dve = (sem(n) for n in ("x_ready", "xt_psum", "xt_act", "xt_dve"))
        proj_psum, proj_evac = sem("proj_psum"), sem("proj_evac")
        s5_step, s5_reduced, s5_sines = sem("s5_step"), sem("s5_reduced"), sem("s5_sines")
        phase_ready, c_ready = sem("phase_ready"), sem("c_ready")
        s5_params = sem("s5_params")
        bu_psum, bu_used, states_ready = sem("bu_psum"), sem("bu_used"), sem("states_ready")
        y_psum, y_sum, y_gelu, glu_psum, glu_sig = (sem(n) for n in ("y_psum", "y_sum", "y_gelu", "glu_psum",
                                                                      "glu_sig"))
        glu_bias = sem("glu_bias")
        sc_psum, sc_evac, sc_max, sc_exp, sc_norm = (sem(n) for n in ("sc_psum", "sc_evac", "sc_max", "sc_exp",
                                                                       "sc_norm"))
        pt_psum, pt_evac, pv_psum, pv_evac = (sem(n) for n in ("pt_psum", "pt_evac", "pv_psum", "pv_evac"))
        conv_done, silu_done, sq_done = sem("conv_done"), sem("silu_done"), sem("sq_done")
        nrm_psum, nrm_ln, nrm_ready, qk_ready = (sem(n) for n in ("nrm_psum", "nrm_ln", "nrm_ready", "qk_ready"))
        turned_back, turned, conv_v = sem("turned_back"), sem("turned"), sem("conv_v")
        m0_ready = sem("m0_ready")
        gate_in, gate_ln, gate_tanh, g_ready, tg_ready = (sem(n) for n in ("gate_in", "gate_ln", "gate_tanh",
                                                                            "g_ready", "tg_ready"))
        nA_exp = sem("nA_exp")
        gs_psum, gs_evac, gs_dve, gs_exp, kd_ready = (sem(n) for n in ("gs_psum", "gs_evac", "gs_dve", "gs_exp",
                                                                        "kd_ready"))
        gb_psum, gb_evac, dt_exp = sem("gb_psum"), sem("gb_evac"), sem("dt_exp")
        kv_psum, kv_evac = sem("kv_psum"), sem("kv_evac")
        kk_psum, la_ready, m_ready = sem("kk_psum"), sem("la_ready"), sem("m_ready")
        u_ready, t_psum, t_ready = sem("u_ready"), sem("t_psum"), sem("t_ready")
        a_psum, a_evac, xy_psum, xy_used = (sem(n) for n in ("a_psum", "a_evac", "xy_psum", "xy_used"))
        up_psum_, up_evac, w_psum, w_evac = (sem(n) for n in ("up_psum", "up_evac", "w_psum", "w_evac"))
        s_zero, ws_psum, qs_psum, vp_ready, su_psum, s_ready, qs_used = (
            sem(n) for n in ("s_zero", "ws_psum", "qs_psum", "vp_ready", "su_psum", "s_ready", "qs_used"))
        av_psum, o_ready, o_sq, o_ss, o_std, og_ready, zw_ready = (
            sem(n) for n in ("av_psum", "o_ready", "o_sq", "o_ss", "o_std", "og_ready", "zw_ready"))
        ot_psum, mix_ready = sem("ot_psum"), sem("mix_ready")
        res_psum, ln_var, ln_std = sem("res_psum"), sem("ln_var"), sem("ln_std")
        xs_hi, xs_lo = sem("xs_hi"), sem("xs_lo")
        gate_silu, h_ready, ht_psum, ht_hi, ht_lo, down_part = (
            sem(n) for n in ("gate_silu", "h_ready", "ht_psum", "ht_hi", "ht_lo", "down_part"))
        lg_psum, gate_exp_in, gate_exp, sel_ready, pos_psum, route_ready = (
            sem(n) for n in ("lg_psum", "gate_exp_in", "gate_exp", "sel_ready", "pos_psum", "route_ready"))
        pick_ready, pickt_psum, pickt_evac = (sem(n) for n in ("pick_ready", "pickt_psum", "pickt_evac"))
        xg_psum, xg_hi, xg_lo, ye_hi, ye_lo, sc_out, sc_added = (
            sem(n) for n in ("xg_psum", "xg_hi", "xg_lo", "ye_hi", "ye_lo", "scatter_psum", "scatter_added"))
        out_ready, out_stored = sem("out_ready"), sem("out_stored")
        dve_step, act_step, pool_step = sem("dve_step"), sem("act_step"), sem("pool_step")

        def at(i, each, n):
            return n if i is None else i * each + (each + n)

        def blocks_of(i):
            return NB if i is None else 1

        AFTER_H = [AT["G", 1, 0]] + [AT["D", j - 1, 0] for j in range(1, FC)]

        def h_bank(i, j):
            return 6 if i is not None else 4 if j else 0

        class Order:

            def __init__(self, eng, s):
                self.eng, self.s, self.n = eng, s, 0

            def __call__(self, ins):
                ins.then_inc(self.s, 1)
                self.n += 1

            def wait(self):
                if self.n:
                    self.eng.wait_ge(self.s, self.n)

            def then(self, ins):
                self(ins)
                self.wait()

        def in_chunk(l, c):
            c0, n = WIN[c]
            return w_in[l].rearrange("(k p) n -> p k n", p=P)[:, :, c0:c0 + n], KT * n

        def tall(w, j):
            return w.rearrange("(k p) n -> p k n", p=P)[:, 4 * j:4 * (j + 1), :]

        def piece(wg_, wu_, wd_, r):
            w, j, p = SEQ[r]
            if w == "D":
                return wd_.rearrange("(k p) n -> p k n", p=P)[:, 4 * j + 2 * p:4 * j + 2 * p + 2, :]
            return (wg_ if w == "G" else wu_).rearrange("(k p) f -> p k f", p=P)[:, 4 * p:4 * p + 4,
                                                                                 512 * j:512 * (j + 1)]

        def tiles_of(t, r):
            return t[:, 0:PIECE].rearrange("p (k n) -> p k n", k=2 if SEQ[r][0] == "D" else 4)

        def slot_wide(s, n=512):
            return slot(s)[:, 0:KT * n].rearrange("p (k n) -> p k n", k=KT)

        def slot_tall(s):
            return slot(s)[:, 0:4096].rearrange("p (k n) -> p k n", k=4)

        block = ctx.enter_context(nc.Block())

        @block.sync
        def _(sp):
            def load_mixer(l):
                for c in range(8):
                    if c >= SLOTS:
                        sp.wait_ge(proj_psum, 13 * l + (2, 4, 6, 8)[c - SLOTS])
                    elif l and c < 3:
                        sp.wait_ge(lo_ready, (NP - 4, NP - 2, NP)[c])
                    elif l:
                        sp.wait_ge(piece_used, AT["U", FC - 1, 1] + 1)
                    dst, src = (slot_wide(c % SLOTS, WIN[c][1]), in_chunk(l, c)[0]) if c < 6 else \
                        (slot_tall(c % SLOTS), tall(w_out[l], c - 6))
                    sp.dma_start(dst, src).then_inc(slot_loaded[c % SLOTS], 16)

            def first_pieces(l, *w):
                for r in range(RAWS):
                    if r < 4:
                        sp.wait_ge(proj_psum, 13 * l + (10, 10, 13, 13)[r])
                    elif r < 6:
                        sp.wait_ge(wo_used, l + 1)
                    else:
                        sp.wait_ge(res_psum, 4 * (l + 1))
                    sp.dma_start(tiles_of(raw[r], r), piece(*w, r)).then_inc(raw_loaded[r], 16)

            def expert_weights(e):
                return [w[0, bass.ds(e, 1)].rearrange("one a b -> (one a) b") for w in (mg, mu, md)]

            def next_piece(i, r, *w):
                if r != RAWS + 1:
                    sp.wait_ge(lo_ready, at(i, NP, r - RAWS + 1 + (r == RAWS)))
                sp.dma_start(tiles_of(raw[r % RAWS], r % NP), piece(*w, r % NP)).then_inc(raw_loaded[r % RAWS], 16)

            def stream(first):
                with sp.Fori(first, first + NE - 1) as i:
                    own, following = expert_weights(i - first), expert_weights(i - (first - 1))
                    for r in range(RAWS, NP + RAWS):
                        next_piece(i, r, *(own if r < NP else following))
                for r in range(RAWS, NP):
                    next_piece(first + NE - 1, r, *expert_weights(NE - 1))

            sp.dma_start(ident, consts[:, 0:P]).then_inc(ident_loaded, 16)
            sp.dma_start(x[:, 0, :], x_in[0, 0:P, :]).then_inc(x_loaded, 16)
            sp.dma_start(x[:, 1, :], x_in[0, P:T, :]).then_inc(x_loaded, 16)
            load_mixer(0)
            dense = (wg[0], wu[0], wd[0])
            first_pieces(0, *dense)
            for r in range(RAWS, NP):
                next_piece(None, r, *dense)
            load_mixer(1)
            first_pieces(1, *expert_weights(0))
            stream(0)
            sp.wait_ge(route_ready, 1)
            most = sp.value_load(count_i[0:1, 0:1], min_val=0, max_val=T)
            with sp.If(most > P):
                for r in range(RAWS):
                    next_piece(NE - 1, NP + r, *expert_weights(0))
                stream(NE)
            for b in range(NB):
                sp.wait_ge(out_ready, b + 1)
                sp.dma_start(out[0, b * P:(b + 1) * P, :], x[:, b, :]).then_inc(out_stored, 16)
            sp.wait_ge(out_stored, 16 * NB)

        def phase_table(eng, step, l):
            tt = eng.tensor_tensor
            pr, pi, qr, qi, t0, t1 = (s5s[:, (12 + k) * 16 + 8 * l:(12 + k) * 16 + 8 * l + 8] for k in range(6))
            step(eng.memset(cos_t[:, :, 0:1], 1.0))
            step(eng.memset(sin_t[:, :, 0:1], 0.0))
            step.wait()
            cur, nxt = (pr, pi), (qr, qi)
            k = 1
            tmp = score_rows[:, 0:2048] if l else zs(O_M, 2048)
            while k < T:
                a = tmp[:, 0:ST * k].rearrange("p (j t) -> p j t", j=ST)
                b = tmp[:, 1024:1024 + ST * k].rearrange("p (j t) -> p j t", j=ST)
                cb = cur[0].unsqueeze(2).to_broadcast([P, ST, k])
                sb_ = cur[1].unsqueeze(2).to_broadcast([P, ST, k])
                step(tt(a, cos_t[:, :, 0:k], cb, ALU.mult))
                step(tt(b, sin_t[:, :, 0:k], sb_, ALU.mult))
                step.wait()
                step(tt(cos_t[:, :, k:2 * k], a, b, ALU.subtract))
                step.wait()
                step(tt(a, cos_t[:, :, 0:k], sb_, ALU.mult))
                step(tt(b, sin_t[:, :, 0:k], cb, ALU.mult))
                if 2 * k < T:
                    step(tt(t0, cur[0], cur[0], ALU.mult))
                    step(tt(t1, cur[1], cur[1], ALU.mult))
                    step(tt(nxt[1], cur[0], cur[1], ALU.mult))
                    step.wait()
                    step(tt(nxt[0], t0, t1, ALU.subtract))
                    step(eng.tensor_scalar(nxt[1], nxt[1], 2.0, None, ALU.mult))
                step.wait()
                last = tt(sin_t[:, :, k:2 * k], a, b, ALU.add)
                if 2 * k < T:
                    step(last)
                    step.wait()
                cur, nxt = nxt, cur
                k *= 2
            last.then_inc(phase_ready, 1)

        def turn_forward(eng, step, t):
            tt = eng.tensor_tensor
            cs = cos_t[:, 4 * t:4 * t + 4, :].rearrange("p j t -> p (j t)")
            sn = sin_t[:, 4 * t:4 * t + 4, :].rearrange("p j t -> p (j t)")
            out_s = [states[r][:, 4 * t:4 * t + 4, :].rearrange("p j t -> p (j t)") for r in range(2)]
            step(tt(mt[0], mt[1], cs, ALU.mult))
            step.then(tt(mt[2], mt[3], sn, ALU.mult))
            step.then(tt(out_s[0], mt[0], mt[2], ALU.subtract))
            step(tt(mt[0], mt[3], cs, ALU.mult))
            step.then(tt(mt[2], mt[1], sn, ALU.mult))
            return tt(out_s[1], mt[0], mt[2], ALU.add)

        @block.gpsimd
        def _(pool):
            step = Order(pool, pool_step)
            pool.dma_start(cst[:, C_REV:CW], consts[:, C_REV:CW]).then_inc(tail_loaded, 16)
            pool.dma_start(par[:, :], params).then_inc(par_loaded, 16)
            pool.wait_ge(slot_loaded[0], 16)
            pool.dma_start(cst[:, P:C_REV], consts[:, P:C_REV]).then_inc(cst_loaded, 16)
            pool.dma_start(b_pad, s5_b[0]).then_inc(b_loaded, 16)
            pool.dma_start(gw, glu_w[0]).then_inc(glu_loaded, 16)
            for l in range(L):
                if l:
                    pool.wait_ge(piece_used, NP)
                    pool.dma_start(b_pad, s5_b[1]).then_inc(b_loaded, 16)
                    pool.dma_start(gw, glu_w[1]).then_inc(glu_loaded, 16)
                pool.wait_ge(turned_back, l + 1)
                pool.wait_ge(phase_ready, l + 1)
                turn_forward(pool, step, 0).then_inc(turned, 1)
                cw = par[:, PO["conv"] + 36 * l:PO["conv"] + 36 * (l + 1)].rearrange("p (c w) -> p c w", c=9)
                for c in range(6, 9):
                    pool.wait_ge(proj_evac, 13 * l + 7 + c // 2)
                    for w in range(4):
                        cb = cw[:, c, w:w + 1].to_broadcast([P, T])
                        if w == 0:
                            step.then(pool.tensor_tensor(qkv[:, c, :], cin[:, c, 0:T], cb, ALU.mult))
                            continue
                        step.then(pool.tensor_tensor(ctmp, cin[:, c, w:w + T], cb, ALU.mult))
                        ins = pool.tensor_tensor(qkv[:, c, :], qkv[:, c, :], ctmp, ALU.add)
                        if (c, w) == (8, 3):
                            ins.then_inc(conv_v, 1)
                        else:
                            step.then(ins)
                pool.wait_ge(pt_psum, NH * (l + 1))
                pool.dma_start(lnrow, ln[2 * l].partition_broadcast(P)).then_inc(ln_loaded, 16)
                for g in range(3):
                    pool.wait_ge(la_ready, 6 * l + 2 * g + 2)
                    ij = slice(4 * g, 4 * g + 4)
                    ins = pool.tensor_tensor(M[1][:, ij, :], LA[:, ij, 1, :],
                                             C("lv1").unsqueeze(1).to_broadcast([P, 4, P]), ALU.mult)
                    if g < 2:
                        step(ins)
                ins.then_inc(m_ready, 1)
                for v in range(2, 6):
                    if v == 2:
                        pool.wait_ge(t_psum, 3 * (l + 1))
                        pool.wait_ge(u_ready, 3 * (l + 1))
                    if v > 2:
                        pool.wait_ge(a_psum, 15 * l + 3 * (v - 2))
                    pool.tensor_tensor(M[v % 2], LA[:, :, 1, :],
                                       C(f"lv{v}").unsqueeze(1).to_broadcast([P, 12, P]), ALU.mult)\
                        .then_inc(m_ready, 1)
                pool.wait_ge(av_psum, NB * (l + 1))
                for r in range(PARTS):
                    pool.wait_ge(hi_ready, (0, NP)[l] + r + 1)
                    pool.tensor_tensor(lo[r][:, :], raw[r], hi[r][:, :].bitcast(F32), ALU.subtract).then_inc(lo_ready, 1)
                pool.wait_ge(x_ready, 2 * NB * l + NB)
                if l == 0:
                    pool.wait_ge(s5_params, 1)
                    phase_table(pool, step, 1)
                    pool.wait_ge(phase_ready, 2)
                pool.dma_start(lnrow, ln[2 * l + 1].partition_broadcast(P)).then_inc(ln_loaded, 16)
            pool.wait_ge(xt_psum, 20)
            pool.wait_ge(xs_lo, 4 + NB)
            pool.tensor_scalar(x, x, ALPHA, None, ALU.mult).then_inc(sc_added, 1)

        @block.scalar
        def _(act):
            af = nc.scalar.activation
            step = Order(act, act_step)

            def high_part(i, r):
                act.wait_ge(raw_loaded[r % RAWS], at(i, 16 * NP // RAWS, 16 * (r // RAWS + 1)))
                if i is not None or r >= PARTS:
                    act.wait_ge(piece_used, at(i, NP, r - PARTS + 1))
                af(hi[r % PARTS][:, :], raw[r % RAWS], ACT.Copy).then_inc(hi_ready, 1)

            def gathered(i):
                act.wait_ge(xg_psum, at(i, 2, 1))
                if i is None:
                    act.wait_ge(lg_psum, 1)
                else:
                    act.wait_ge(piece_used, at(i, NP, AT["U", FC - 1, 1] + 1))
                af(xg[0][:, :], ps[:, 2:4, :].rearrange("p a n -> p (a n)"), ACT.Copy).then_inc(xg_hi, 1)

            def channel_mixer(i, more):
                nb = blocks_of(i)
                hT = hT_d if i is None else hT_e
                for r in range(NP):
                    w, j, p = SEQ[r]
                    if r == NP - 1 and i is not None:
                        for c in range(2):
                            if c == 0:
                                act.wait_ge(down_part, i + 4)
                            else:
                                act.wait_ge(piece_used, at(i, NP, NP))
                            af(ye[0][:, 512 * c:512 * (c + 1)], ps[:, c, :], ACT.Copy).then_inc(ye_hi, 1)
                    if r + PARTS < NP:
                        high_part(i, r + PARTS)
                    elif more:
                        high_part(i + 1, r + PARTS - NP)
                    if (w, p) == ("G", 1):
                        act.wait_ge(piece_used, at(i, NP, r + 1))
                        if j:
                            act.wait_ge(h_ready, at(i, FC, j))
                        af(sg[:, 0:512 * nb], ps[:, 4:4 + nb, :].rearrange("p a n -> p (a n)"),
                           ACT.Silu).then_inc(gate_silu, 1)
                    if r in AFTER_H:
                        j = AFTER_H.index(r)
                        act.wait_ge(ht_psum, at(i, FC, j + 1))
                        src = ps[:, h_bank(i, j):h_bank(i, j) + nb, :].rearrange("p a n -> p (a n)")
                        af(hT[j % 2][0][:, :], src, ACT.Copy).then_inc(ht_hi, 1)
                    if i is not None and r == AT["G", 1, 1]:
                        act.wait_ge(pickt_psum, i + 1)
                        af(pickT[:, :], ps[:, 7, 0:T], ACT.Copy).then_inc(pickt_evac, 1)
                    if i is not None and r == AT["U", FC - 1, 1]:
                        gathered(i)

            for l in range(L):
                n_x = 2 * l
                for q in range(2):
                    act.wait_ge(xt_psum, 4 * n_x + q + 1)
                    af(xT[:, 2 * q:2 * q + 2, :], ps[:, q, :], ACT.Copy).then_inc(xt_act, 1)
                if l == 0:
                    act.wait_ge(par_loaded, 16)
                    af(s5s[:, 0:16], par[:, PO["ldt"]:PO["ldt"] + 16], ACT.Exp).then_inc(s5_step, 1)
                    af(nA, par[:, PO["alog"]:PO["alog"] + 12], ACT.Exp).then_inc(nA_exp, 1)
                    act.wait_ge(tail_loaded, 16)
                    act.wait_ge(s5_reduced, 1)
                    af(s5s[:, 32:48], s5s[:, 64:80], ACT.Sin).then_inc(s5_sines, 1)
                    af(s5s[:, 48:64], s5s[:, 80:96], ACT.Sin, bias=cst[:, C_HPI:C_HPI + 1], scale=-1.0)\
                        .then_inc(s5_sines, 1)

                def evac(n, *pairs):
                    act.wait_ge(proj_psum, 13 * l + n + 1)
                    for k, (dst, src) in enumerate(pairs):
                        ins = af(dst, src, ACT.Copy)
                        if k == len(pairs) - 1:
                            ins.then_inc(proj_evac, 1)
                        else:
                            step(ins)

                if l:
                    act.wait_ge(x_ready, 4)
                evac(0, (uT, ps[:, 4, :]))
                evac(1, (qkm[:, 0:2, :], ps[:, 5, :]))
                evac(2, (qkm[:, 2:4, :], ps[:, 2, :]))
                evac(3, (qkm[:, 4:6, :], ps[:, 3, :]))
                evac(4, (mv[:, 0, :], ps[:, 4, 0:384]))
                evac(5, (mv[:, 1, :], ps[:, 5, 0:384]))
                evac(6, (cin[:, 0:2, 3:259], ps[:, 6, :].rearrange("p (a t) -> p a t", a=2)))
                evac(7, (cin[:, 2:4, 3:259], ps[:, 7, :].rearrange("p (a t) -> p a t", a=2)))
                act.wait_ge(sc_max, l + 1)
                for h in range(NH):
                    for b, (c0, n) in enumerate(((0, P), (P, T))):
                        af(sc[:, h, c0:c0 + n], sc[:, h, c0:c0 + n], ACT.Exp, bias=nmax[:, 6 * b + h:6 * b + h + 1],
                           accum_out=rsum[:, 6 * b + h:6 * b + h + 1]).then_inc(sc_exp, 1)
                evac(8, (cin[:, 4:6, 3:259], ps[:, 0, :].rearrange("p (a t) -> p a t", a=2)))
                evac(9, (cin[:, 6:8, 3:259], ps[:, 1, :].rearrange("p (a t) -> p a t", a=2)))
                evac(10, (cin[:, 8, 3:259], ps[:, 4, 0:T]))
                for b, bank in ((0, 5), (1, 2)):
                    act.wait_ge(proj_psum, 13 * l + 12 + b)
                    step(af(ab[:, b, :], ps[:, bank, 384:396], ACT.Copy))
                    af(zt[:, b, :], ps[:, bank, 0:384], ACT.Silu).then_inc(proj_evac, 1)
                for c in range(3):
                    if c == 2:
                        act.wait_ge(silu_done, 3 * l + 2)
                        act.wait_ge(states_ready, l + 1)
                        af(sq, qkv[:, 0:6, :], ACT.Square).then_inc(sq_done, 1)
                        for h in range(NH):
                            act.wait_ge(pt_psum, NH * l + h + 1)
                            af(pT[:, h, :], ps[:, (7, 0)[h % 2], 0:384], ACT.Copy).then_inc(pt_evac, 1)
                    act.wait_ge(conv_done, 2 * l + c + 1) if c < 2 else act.wait_ge(conv_v, l + 1)
                    af(qkv[:, 3 * c:3 * c + 3, :], qkv[:, 3 * c:3 * c + 3, :], ACT.Silu).then_inc(silu_done, 1)
                act.wait_ge(y_sum, l + 1)
                af(ys, ys, ACT.Gelu_apprx_tanh).then_inc(y_gelu, 1)
                act.wait_ge(gate_in, l + 1)
                af(l1, l1, ACT.Exp, scale=-1.0).then_inc(gate_ln, 1)
                act.wait_ge(gate_ln, 2 * l + 1)
                af(l1, l1, ACT.Ln, bias=cst[:, C_ONE:C_ONE + 1]).then_inc(gate_ln, 1)
                for q, bank in enumerate((2, 3, 6)):
                    act.wait_ge(nrm_psum, 3 * l + q + 1)
                    af(rn[:, 2 * q:2 * q + 2, :], ps[:, bank, :], ACT.Ln, bias=cst[:, C_EPS6:C_EPS6 + 1])\
                        .then_inc(nrm_ln, 1)
                act.wait_ge(nrm_ln, 3 * (l + 1))
                af(rn, rn, ACT.Exp, scale=-0.5).then_inc(nrm_ready, 1)
                act.wait_ge(proj_evac, 13 * (l + 1))
                af(by_bh(beta), ab[:, :, 6:12].rearrange("p b (j r) -> p b j r", j=3), ACT.Tanh, scale=0.5)\
                    .then_inc(gate_tanh, 1)
                act.wait_ge(glu_psum, l + 1)
                act.wait_ge(glu_bias, 1)
                for f in range(2):
                    af(sig[:, f, :], ps[:, 7, f * T:(f + 1) * T], ACT.Tanh, bias=gbh[:, 2 * l + f:2 * l + f + 1],
                       scale=0.5).then_inc(glu_sig, 1)
                act.wait_ge(gs_psum, l + 1)
                af(gsum, ps[:, 5, 0:48], ACT.Copy).then_inc(gs_evac, 1)
                act.wait_ge(gs_evac, l + 1)
                af(eg, gsum[:, 0:12], ACT.Exp).then_inc(gs_exp, 1)
                af(eS, gsum[:, 24:48], ACT.Exp).then_inc(gs_exp, 1)
                act.wait_ge(gs_dve, l + 1)
                af(ekl, ekl, ACT.Exp).then_inc(gs_exp, 1)
                act.wait_ge(gb_evac, 3 * (l + 1))
                for i in range(12):
                    af(dt_[:, i, :], dt_[:, i, :], ACT.Exp, bias=ngc[:, i:i + 1]).then_inc(dt_exp, 1)
                for q, bank in enumerate((4, 5, 2)):
                    act.wait_ge(kv_psum, 3 * l + q + 1)
                    dst = zf(O_KV + 512 * q, 512)
                    af(dst, ps[:, bank, :], ACT.Copy).then_inc(kv_evac, 1)
                for n in range(15):
                    act.wait_ge(a_psum, 15 * l + n + 1)
                    g = n % 3
                    if n >= 3:
                        act.wait_ge(xy_psum, 15 * l + n - 2)
                    af(A[:, 4 * g:4 * g + 4, :], ps[:, (2, 5)[n % 2], :], ACT.Copy).then_inc(a_evac, 1)
                for q in range(2):
                    act.wait_ge(w_psum, 2 * l + q + 1)
                    af(wT[:, 2 * q:2 * q + 2 - q, :], ps[:, q, 0:512 - 256 * q], ACT.Copy).then_inc(w_evac, 1)
                for b in range(NB):
                    act.wait_ge(o_ready, NB * l + b + 1)
                    af(osq[:, b, :], o[:, b, :], ACT.Square).then_inc(o_sq, 1)
                    act.wait_ge(o_ss, NB * l + b + 1)
                    af(ss[:, 6 * b:6 * b + 6], ss[:, 6 * b:6 * b + 6], ACT.Sqrt, bias=cst[:, C_EPS6:C_EPS6 + 1],
                       scale=1.0 / HD).then_inc(o_std, 1)

                def norm(n):
                    for b in range(NB):
                        act.wait_ge(ln_var, NB * n + b + 1)
                        af(std[:, b:b + 1], mvar[:, 1:2], ACT.Sqrt, bias=cst[:, C_EPS5:C_EPS5 + 1])\
                            .then_inc(ln_std, 1)

                act.wait_ge(up_psum_, NB * (l + 1))
                for r in range(PARTS):
                    high_part(None if l == 0 else 0, r)
                norm(2 * l)
                if l == 0:
                    for q in range(4):
                        act.wait_ge(xt_psum, 4 * (n_x + 1) + q + 1)
                        af(xs_x[0][:, 2 * q:2 * q + 2, :], ps[:, (4, 3, 6, 7)[q], :], ACT.Copy).then_inc(xs_hi, 1)
                    channel_mixer(None, False)
                    norm(1)
            for b in range(NB):
                act.wait_ge(x_ready, 2 * NB + b + 1)
                af(xs[0][:, b * D:(b + 1) * D], x[:, b, :], ACT.Copy).then_inc(xs_hi, 1)
                for q in range(4 - 2 * b):
                    act.wait_ge(xt_psum, 12 + 4 * b + q + 1)
                    af(xT[:, 2 * q:2 * q + 2, b * P:(b + 1) * P],
                       ps[:, (4, 3, 6, 7)[q], :].rearrange("p (k t) -> p k t", k=2)[:, :, b * P:(b + 1) * P],
                       ACT.Copy).then_inc(xt_act, 1)
            act.wait_ge(gate_exp_in, 1)
            af(rt[:, 100:102], rt[:, 98:100], ACT.Exp).then_inc(gate_exp, 1)
            gathered(None)
            with act.Fori(0, NE - 1) as i:
                channel_mixer(i, True)
            channel_mixer(NE - 1, False)
            act.wait_ge(route_ready, 1)
            most = act.value_load(count_i[0:1, 0:1], min_val=0, max_val=T)
            with act.If(most > P):
                for r in range(PARTS):
                    high_part(NE, r)
                with act.Fori(NE, 2 * NE - 1) as i:
                    channel_mixer(i, True)
                channel_mixer(2 * NE - 1, False)
            for b in range(NB):
                act.wait_ge(ln_var, NB * 3 + b + 1)
                af(std[:, b:b + 1], mvar[:, 1:2], ACT.Sqrt, bias=cst[:, C_EPS5:C_EPS5 + 1]).then_inc(ln_std, 1)

        @block.vector
        def _(dve):
            v_ = nc.vector
            tt, ts, stt = v_.tensor_tensor, v_.tensor_scalar, v_.scalar_tensor_tensor
            step = Order(dve, dve_step)

            def pc(name, l, n):
                return par[:, PO[name] + l * n:PO[name] + (l + 1) * n]

            def s5_parameters():
                N = L * ST
                sv = [s5s[:, N * k:N * (k + 1)] for k in range(24)]
                st, _, sh, ch, half, ahalf, a, th, w, e, k_, t0, pr, pi, _, _, t1, t2 = sv[:18]
                fr, fi, rad, den, xr, xi = sv[18:24]
                lre, lim = par[:, PO["lre"]:PO["lre"] + N], par[:, PO["lim"]:PO["lim"] + N]
                dve.wait_ge(s5_step, 1)
                step(tt(a, lre, st, ALU.mult))
                step.then(tt(th, lim, st, ALU.mult))
                big = 1.5 * 2.0 ** 23
                step.then(ts(k_, th, float(1 / (2 * np.pi)), big, ALU.mult, ALU.add))
                step.then(ts(k_, k_, -big, None, ALU.add))
                c1 = 6.28125
                c2 = float(np.float32(np.floor((2 * np.pi - c1) * 2 ** 20) / 2 ** 20))
                c3 = float(2 * np.pi - c1 - c2)
                for c in (c1, c2, c3):
                    step.then(stt(th, k_, -c, th, ALU.mult, ALU.add))
                step.then(ts(half, th, 0.5, float(np.float32(1.5707963)), ALU.mult, ALU.min))
                step.then(ts(half, half, -float(np.float32(1.5707963)), None, ALU.max))
                stt(ahalf, half, -1.0, half, ALU.mult, ALU.max).then_inc(s5_reduced, 1)
                step.then(ts(w, a, -100.0, 88.0, ALU.max, ALU.min))
                step.then(ts(w, w, 1.0 / 128, None, ALU.mult))
                fact = 3628800.0
                step.then(ts(e, w, 1.0 / fact, None, ALU.mult))
                for n in range(9, 0, -1):
                    fact = fact / (n + 1)
                    step.then(stt(e, e, 1.0 / fact, w, ALU.add, ALU.mult))
                for _i in range(7):
                    step.then(stt(e, e, 2.0, e, ALU.add, ALU.mult))
                step(ts(rad, e, 1.0, None, ALU.add))
                dve.wait_ge(s5_sines, 2)
                step.then(tt(t0, sh, sh, ALU.mult))
                step.then(ts(t0, t0, -2.0, None, ALU.mult))
                step(ts(pr, t0, 1.0, None, ALU.add))
                step.then(stt(pi, sh, 2.0, ch, ALU.mult, ALU.mult))
                step.then(tt(t1, e, pr, ALU.mult))
                step(tt(xr, t1, t0, ALU.add))
                step.then(tt(xi, rad, pi, ALU.mult))
                step(tt(t1, lre, lre, ALU.mult))
                step.then(tt(t2, lim, lim, ALU.mult))
                step.then(tt(den, t1, t2, ALU.add))
                step.then(v_.reciprocal(den, den))
                step(tt(t1, xr, lre, ALU.mult))
                step.then(tt(t2, xi, lim, ALU.mult))
                step.then(tt(t1, t1, t2, ALU.add))
                step.then(tt(fr, t1, den, ALU.mult))
                step(tt(t1, xi, lre, ALU.mult))
                step.then(tt(t2, xr, lim, ALU.mult))
                step.then(tt(t1, t1, t2, ALU.subtract))
                tt(fi, t1, den, ALU.mult).then_inc(s5_params, 1)
                dve.wait_ge(s5_params, 1)
                ts(gbh[:, :], par[:, PO["gb"]:PO["gb"] + 4], 0.5, None, ALU.mult).then_inc(glu_bias, 1)
                dve.wait_ge(nA_exp, 1)
                step.then(ts(nA, nA, -1.0, None, ALU.mult))

            def c_padded(l):
                cc = par[:, PO["c"] + 256 * l:PO["c"] + 256 * (l + 1)].rearrange("p (j r f) -> p j r f", j=ST, r=2)
                fr, fi = (s5s[:, 16 * k + 8 * l:16 * k + 8 * l + 8].unsqueeze(2).to_broadcast([P, ST, 16])
                          for k in (18, 19))
                t = [mt[0][:, 128 * k:128 * (k + 1)].rearrange("p (j f) -> p j f", j=ST) for k in range(4)]
                step(v_.memset(c_pad, 0.0))
                step(tt(t[0], cc[:, :, 0, :], fr, ALU.mult))
                step(tt(t[1], cc[:, :, 1, :], fi, ALU.mult))
                step(tt(t[2], cc[:, :, 1, :], fr, ALU.mult))
                step.then(tt(t[3], cc[:, :, 0, :], fi, ALU.mult))
                for half in range(2):
                    rows = slice(64 * half, 64 * half + 64)
                    for q in range(4):
                        f0 = 32 * q + 16 * half
                        step(tt(c_pad[rows, q::4, 0, f0:f0 + 16], t[0][rows, q::4], t[1][rows, q::4], ALU.subtract))
                        ins = stt(c_pad[rows, q::4, 1, f0:f0 + 16], t[2][rows, q::4], -1.0, t[3][rows, q::4],
                                  ALU.mult, ALU.subtract)
                        if (half, q) != (1, 3):
                            step(ins)
                ins.then_inc(c_ready, 1)
                dve.wait_ge(c_ready, l + 1)
                step.wait()

            def s5_scan(l, t):
                re, im = ((6, 0), (6, 2))[t]
                cs = cos_t[:, 4 * t:4 * t + 4, :].rearrange("p (a j) t -> p a (j t)", a=2)
                sn = sin_t[:, 4 * t:4 * t + 4, :].rearrange("p (a j) t -> p a (j t)", a=2)
                v3 = [m.rearrange("p (a n) -> p a n", a=2) for m in mt]
                if t:
                    dve.wait_ge(turned, l + 1)
                dve.wait_ge(bu_psum, 2 * l + t + 1)
                step(tt(v3[0], ps[:, re:re + 2, :], cs, ALU.mult))
                step(tt(v3[1], ps[:, im:im + 2, :], sn, ALU.mult))
                step(tt(v3[2], ps[:, im:im + 2, :], cs, ALU.mult))
                tt(v3[3], ps[:, re:re + 2, :], sn, ALU.mult).then_inc(bu_used, 1)
                dve.wait_ge(bu_used, 2 * l + t + 1)
                step.wait()
                step(tt(mt[0], mt[0], mt[1], ALU.add))
                step.then(tt(mt[2], mt[2], mt[3], ALU.subtract))
                for jj in range(4):
                    r0 = 16 * 20 + 8 * l + 4 * t + jj
                    rad = s5s[:, r0:r0 + 1].to_broadcast([P, T])
                    for k in range(2):
                        ins = v_.tensor_tensor_scan(mt[2 * k + 1][:, jj * T:(jj + 1) * T], rad,
                                                    mt[2 * k][:, jj * T:(jj + 1) * T], 0.0, ALU.mult, ALU.add)
                        if (jj, k, t) == (3, 1, 0):
                            ins.then_inc(turned_back, 1)
                        else:
                            step(ins)
                if t:
                    step.wait()
                    turn_forward(v_, step, 1).then_inc(states_ready, 1)
                    dve.wait_ge(states_ready, l + 1)

            def norm(n, banks, sum_of):
                for b in range(NB):
                    dve.wait_ge(ln_loaded, 16 * (n + 1))
                    for c in range(2):
                        xc = x[:, b, 512 * c:512 * (c + 1)]
                        if banks is not None:
                            sum_of(2 * b + c)
                            step.then(stt(xc, xc, ALPHA, ps[:, banks[2 * b + c], :], ALU.mult, ALU.add))
                        step(v_.bn_stats(stats[:, 6 * c:6 * c + 6], xc))
                    step.wait()
                    if b:
                        dve.wait_ge(ln_std, NB * n + b)
                    v_.bn_aggr(mvar, stats).then_inc(ln_var, 1)
                    dve.wait_ge(ln_var, NB * n + b + 1)
                    step.then(stt(x[:, b, :], x[:, b, :], mvar[:, 0:1], lnrow[:, 0, :], ALU.subtract, ALU.mult))
                    dve.wait_ge(ln_std, NB * n + b + 1)
                    step.then(v_.reciprocal(rstd, std[:, b:b + 1]))
                    s_done = out_ready if n == 3 else x_ready
                    stt(x[:, b, :], x[:, b, :], rstd, lnrow[:, 1, :], ALU.mult, ALU.add).then_inc(s_done, 1)
                    dve.wait_ge(s_done, (0 if n == 3 else NB * n) + b + 1)

            def x_transposed(n, banks):
                for q in range(2, 4):
                    dve.wait_ge(xt_psum, 4 * n + q + 1)
                    v_.tensor_copy(xT[:, 2 * q:2 * q + 2, :], ps[:, banks[q], :]).then_inc(xt_dve, 1)

            def low_part(i, r):
                if i is None and r == PARTS:
                    dve.wait_ge(lo_ready, PARTS)
                dve.wait_ge(hi_ready, at(i, NP, r + 1))
                tt(lo[r % PARTS][:, :], raw[r % RAWS], hi[r % PARTS][:, :].bitcast(F32), ALU.subtract)\
                    .then_inc(lo_ready, 1)

            def pick_tokens(i):
                for b in range(NB):
                    where = pos[:, b, i:i + 1] if isinstance(i, int) else pos[:, b, bass.ds(i, 1)]
                    ts(pick[:, b, :], C("iota"), where, None, ALU.is_equal).then_inc(pick_ready, 1)

            def gathered(i):
                dve.wait_ge(xg_psum, at(i, 2, 2))
                bank = 6 if i is None else 2
                v_.tensor_copy(xg[1][:, :], ps[:, bank:bank + 2, :].rearrange("p a n -> p (a n)")).then_inc(xg_lo, 1)

            def channel_mixer(i, more):
                nb = blocks_of(i)
                hT = hT_d if i is None else hT_e

                def low_ahead(r):
                    if r + PARTS < NP:
                        low_part(i, r + PARTS)
                    elif more:
                        low_part(i + 1, r + PARTS - NP)

                for r in range(NP):
                    w, j, p = SEQ[r]
                    if (w, p) == ("U", 1):
                        dve.wait_ge(piece_used, at(i, NP, r + 1))
                        dve.wait_ge(gate_silu, at(i, FC, j + 1))
                        if j:
                            dve.wait_ge(ht_psum, at(i, FC, j))
                        tt(hh[:, 0:512 * nb], ps[:, 4 + nb:4 + 2 * nb, :].rearrange("p a n -> p (a n)"),
                           sg[:, 0:512 * nb], ALU.mult).then_inc(h_ready, 1)
                    if r == NP - 1 and i is not None:
                        for c in range(2):
                            dve.wait_ge(ye_hi, i * 2 + (c + 1))
                            half = slice(512 * c, 512 * (c + 1))
                            tt(ye[1][:, half], ps[:, c, :], ye[0][:, half].bitcast(F32), ALU.subtract)\
                                .then_inc(ye_lo, 1)
                        for k, bank in enumerate((2, 3, 7, 6)):
                            c, b = divmod(k, 2)
                            if k == 2:
                                low_ahead(r)
                            dve.wait_ge(sc_out, i * 4 + (k + 1))
                            xc = x[:, b, 512 * c:512 * (c + 1)]
                            stt(xc, ps[:, bank, :], comb[:, b, i:i + 1] if isinstance(i, int) else
                                comb[:, b, bass.ds(i, 1)], xc, ALU.mult, ALU.add).then_inc(sc_added, 1)
                        dve.wait_ge(sc_added, i * 4 + 5)
                    else:
                        low_ahead(r)
                    if r in AFTER_H:
                        j = AFTER_H.index(r)
                        dve.wait_ge(ht_hi, at(i, FC, j + 1))
                        src = ps[:, h_bank(i, j):h_bank(i, j) + nb, :].rearrange("p a n -> p (a n)")
                        tt(hT[j % 2][1][:, :], src, hT[j % 2][0][:, :].bitcast(F32), ALU.subtract)\
                            .then_inc(ht_lo, 1)
                    if i is not None and r == AT["G", 1, 1]:
                        dve.wait_ge(pickt_psum, i + 1)
                        pick_tokens(i + 1)
                    if i is not None and r == AT["D", FC - 2, 1]:
                        gathered(i)

            for l in range(L):
                x_transposed(2 * l, (0, 1, 6, 7))
                if l == 0:
                    dve.wait_ge(par_loaded, 16)
                    s5_parameters()
                    phase_table(v_, step, 0)
                    dve.wait_ge(phase_ready, 1)
                else:
                    dve.wait_ge(phase_ready, 2)
                dve.wait_ge(cst_loaded, 16)
                c_padded(l)
                step(v_.memset(cin[:, :, 0:3], 0.0))
                s5_scan(l, 0)
                for h in range(NH):
                    bank = (2, 3, 0, 1, 4, 5)[h]
                    dve.wait_ge(sc_psum, NH * l + h + 1)
                    step(stt(sc[:, h, 0:P], ps[:, bank, 0:P], SCALE, C("causal"), ALU.mult, ALU.add))
                    step(ts(sc[:, h, P:2 * P], ps[:, bank, P:2 * P], SCALE, None, ALU.mult))
                    stt(sc[:, h, 2 * P:3 * P], ps[:, bank, 2 * P:3 * P], SCALE, C("causal"), ALU.mult, ALU.add)\
                        .then_inc(sc_evac, 1)
                dve.wait_ge(sc_evac, NH * (l + 1))
                step.wait()
                step(v_.tensor_reduce(nmax[:, 0:6], sc[:, :, 0:P], AX_X, ALU.max))
                step.then(v_.tensor_reduce(nmax[:, 6:12], sc[:, :, P:3 * P], AX_X, ALU.max))
                ts(nmax, nmax, -1.0, None, ALU.mult).then_inc(sc_max, 1)
                s5_scan(l, 1)
                dve.wait_ge(sc_exp, 2 * NH * (l + 1))
                step.then(v_.reciprocal(rinv, rsum))
                for b, (c0, n) in enumerate(((0, P), (P, T))):
                    tt(sc[:, :, c0:c0 + n], sc[:, :, c0:c0 + n],
                       rinv[:, 6 * b:6 * b + 6].unsqueeze(2).to_broadcast([P, NH, n]), ALU.mult)\
                        .then_inc(sc_norm, 1)
                cw = par[:, PO["conv"] + 36 * l:PO["conv"] + 36 * (l + 1)].rearrange("p (c w) -> p c w", c=9)
                for c in range(6):
                    if c % 2 == 0:
                        dve.wait_ge(proj_evac, 13 * l + 7 + c // 2)
                    step.then(ts(qkv[:, c, :], cin[:, c, 0:T], cw[:, c, 0:1], None, ALU.mult))
                    for w in range(1, 4):
                        ins = stt(qkv[:, c, :], cin[:, c, w:w + T], cw[:, c, w:w + 1], qkv[:, c, :],
                                  ALU.mult, ALU.add)
                        if w == 3 and c % 3 == 2:
                            ins.then_inc(conv_done, 1)
                        else:
                            step.then(ins)
                dve.wait_ge(proj_evac, 13 * (l + 1))
                x3 = xx.rearrange("p (b h) -> p b h", b=2)
                step.then(tt(x3, ab[:, :, 0:6], pc("dtb", l, NH).unsqueeze(1).to_broadcast([P, 2, NH]), ALU.add))
                stt(l1, xx, -1.0, xx, ALU.mult, ALU.max).then_inc(gate_in, 1)
                dve.wait_ge(y_psum, l + 1)
                for f in range(2):
                    stt_out = stt(ys[:, f, :], uT[:, f, :], par[:, PO["d"] + 2 * l + f:PO["d"] + 2 * l + f + 1],
                                  ps[:, 3, f * T:(f + 1) * T], ALU.mult, ALU.add)
                    if f:
                        stt_out.then_inc(y_sum, 1)
                    else:
                        step.then(stt_out)
                dve.wait_ge(gate_ln, 2 * (l + 1))
                step.then(stt(xx, xx, 0.0, l1, ALU.max, ALU.add))
                na = nA[:, NH * l:NH * (l + 1)].unsqueeze(1).to_broadcast([P, 2, NH])
                step.then(tt(x3, x3, na, ALU.mult))
                v_.tensor_copy(by_bh(g_i), xx.rearrange("p (b j r) -> p b j r", b=2, j=3)).then_inc(g_ready, 1)
                dve.wait_ge(g_ready, l + 1)
                tt(tg, C("cum").unsqueeze(1).to_broadcast([P, 12, P]), g_i.unsqueeze(2).to_broadcast([P, 12, P]),
                   ALU.mult).then_inc(tg_ready, 1)
                dve.wait_ge(pv_psum, l + 1)
                step(v_.tensor_copy(xT[:, 2:4, :], ps[:, 1, :]))
                v_.tensor_copy(xT[:, 4, :], ps[:, 4, 0:T]).then_inc(pv_evac, 1)
                dve.wait_ge(nrm_ready, l + 1)
                step(stt(qkv[:, 0:3, :], qkv[:, 0:3, :], SCALE, rn[:, 0:3, :], ALU.mult, ALU.mult))
                tt(qkv[:, 3:6, :], qkv[:, 3:6, :], rn[:, 3:6, :], ALU.mult).then_inc(qk_ready, 1)
                dve.wait_ge(gate_tanh, l + 1)
                step(ts(beta, beta, 0.5, 0.5, ALU.mult, ALU.add))
                dve.wait_ge(glu_sig, 2 * (l + 1))
                step.then(stt(sig, sig, 1.0, ys, ALU.add, ALU.mult))
                ts(xT[:, 0:2, :], sig, 0.5, None, ALU.mult).then_inc(mix_ready, 1)
                dve.wait_ge(gs_evac, l + 1)
                step(ts(ngc, gsum[:, 0:12], -1.0, None, ALU.mult))
                tt(ekl, gsum[:, 12:24], gsum[:, 0:12], ALU.subtract).then_inc(gs_dve, 1)
                for q, bank in enumerate((7, 0, 1)):
                    dve.wait_ge(gb_psum, 3 * l + q + 1)
                    tt(dt_[:, 4 * q:4 * q + 4, :], ps[:, bank, :].rearrange("p (i c) -> p i c", i=4),
                       C("negu").unsqueeze(1).to_broadcast([P, 4, P]), ALU.add).then_inc(gb_evac, 1)
                idb = ident.unsqueeze(1)
                dve.wait_ge(dt_exp, 12 * (l + 1))
                step.then(tt(dt_, dt_, beta.unsqueeze(2).to_broadcast([P, 12, P]), ALU.mult))
                for q, bank in enumerate((3, 6, 7, 0, 1, 4)):
                    dve.wait_ge(kk_psum, 6 * l + q + 1)
                    ij = slice(2 * q, 2 * q + 2)
                    tt(LA[:, 2 * q:2 * q + 2], ps[:, bank, :].rearrange("p (i w c) -> p i w c", i=2, w=2),
                       dt_[:, 2 * q:2 * q + 2, :].unsqueeze(2).to_broadcast([P, 2, 2, P]), ALU.mult)\
                        .then_inc(la_ready, 1)
                    dve.wait_ge(la_ready, 6 * l + q + 1)
                    tt(M[0][:, ij, :], LA[:, ij, 1, :], C("lv0").unsqueeze(1).to_broadcast([P, 2, P]), ALU.mult)\
                        .then_inc(m0_ready, 1)
                for g in range(3):
                    ij = slice(4 * g, 4 * g + 4)
                    dve.wait_ge(m0_ready, 6 * l + 2 * g + 2)
                    tt(U[:, ij, :], idb.to_broadcast([P, 4, P]), M[0][:, ij, :], ALU.subtract).then_inc(u_ready, 1)
                    dve.wait_ge(t_psum, 3 * l + g + 1)
                    tt(Tm[:, 4 * g:4 * g + 4, :], idb.to_broadcast([P, 4, P]),
                       ps[:, (0, 1, 3)[g], :].rearrange("p (i c) -> p i c", i=4), ALU.subtract).then_inc(t_ready, 1)
                dve.wait_ge(kv_evac, 3 * (l + 1))
                dve.wait_ge(gs_exp, 3 * (l + 1))
                step.wait()
                step.then(tt(ekl, ekl, beta, ALU.mult))
                for b in range(NB):
                    for dst, by in ((kg, eg), (kd, ekl)):
                        h4 = "p (j r d) -> p j r d"
                        step(tt(dst[:, b, :].rearrange(h4, j=3, r=2), kv[:, 0, b, :].rearrange(h4, j=3, r=2),
                                by_bh(by)[:, b].unsqueeze(3).to_broadcast([P, 3, 2, HD]), ALU.mult))
                step(tt(zt.rearrange("p b (h d) -> p (b h) d", h=NH), zt.rearrange("p b (h d) -> p (b h) d", h=NH),
                        pc("nw", l, HD).unsqueeze(1).to_broadcast([P, 12, HD]), ALU.mult))
                step.wait()
                v_.memset(S, 0.0).then_inc(s_zero, 1)
                for v in range(5):
                    for g in range(3):
                        n = 3 * v + g
                        i4 = slice(4 * g, 4 * g + 4)
                        dve.wait_ge(xy_psum, 15 * l + n + 1)
                        if v < 4:
                            step(tt(Tm[:, i4, :], Tm[:, i4, :], ps[:, (0, 1, 3)[g], :]
                                    .rearrange("p (i c) -> p i c", i=4), ALU.subtract))
                        step.wait()
                        tt(U[:, i4, :], U[:, i4, :], ps[:, (4, 6, 7)[g], :].rearrange("p (i c) -> p i c", i=4),
                           ALU.subtract).then_inc(xy_used, 1)
                for b in range(NB):
                    dve.wait_ge(up_psum_, NB * l + b + 1)
                    v_.tensor_copy(up[:, b, :], ps[:, (2, 5)[b], 0:384]).then_inc(up_evac, 1)

                def mixed(b):
                    dve.wait_ge(ot_psum, NB * l + b + 1)
                    v_.tensor_copy(xT[:, 5:8, b * P:(b + 1) * P],
                                   ps[:, 3 + b, 0:384].rearrange("p (j t) -> p j t", j=3)).then_inc(mix_ready, 1)

                for n in range(NC):
                    b, c = divmod(n, 2)
                    rows = slice(64 * c, 64 * c + 64)
                    dve.wait_ge(up_evac, NB * (l + 1))
                    dve.wait_ge(ws_psum, NC * l + n + 1)
                    tt(vp[rows, b, :], up[rows, b, :], ps[rows, 3, 0:384], ALU.subtract).then_inc(vp_ready, 1)
                    dve.wait_ge(qs_psum, NC * l + n + 1)
                    for r in range(2 if n < NC - 1 else 0):
                        hr = slice(64 * r, 64 * r + 64)
                        by = eS.rearrange("p (c r j b) -> p c b r j", c=2, r=2, j=3)[hr, c, b, r]
                        step(tt(S[hr, :, hr], S[hr, :, hr], by.unsqueeze(2).to_broadcast([64, 3, HD]), ALU.mult))
                    tt(o[rows, b, :].rearrange("p (j r d) -> p j r d", j=3, r=2),
                       ps[rows, 4, 0:384].rearrange("p (j r d) -> p j r d", j=3, r=2),
                       by_bh(eg)[rows, b].unsqueeze(3).to_broadcast([64, 3, 2, HD]), ALU.mult).then_inc(qs_used, 1)
                    if n < NC - 1:
                        dve.wait_ge(su_psum, (NC - 1) * l + n + 1)
                        step.wait()
                    for r in range(2 if n < NC - 1 else 0):
                        hr = slice(64 * r, 64 * r + 64)
                        tt(S[hr, :, hr], S[hr, :, hr],
                           ps[hr, 6, 0:384].rearrange("p (j e) -> p j e", j=3)[:, :, hr], ALU.add)\
                            .then_inc(s_ready, 1)
                    if c:
                        dve.wait_ge(qs_used, NC * l + n + 1)
                        dve.wait_ge(av_psum, NB * l + b + 1)
                        tt(o[:, b, :], o[:, b, :], ps[:, 7, 0:384], ALU.add).then_inc(o_ready, 1)
                    if n < NC - 1:
                        dve.wait_ge(s_ready, 2 * ((NC - 1) * l + n + 1))
                    if n == NC - 1:
                        mixed(0)
                    if n < 2:
                        continue
                    b = n - 2
                    o3 = o[:, b, :].rearrange("p (h d) -> p h d", h=NH)
                    dve.wait_ge(o_sq, NB * l + b + 1)
                    v_.tensor_reduce(ss[:, 6 * b:6 * b + 6], osq[:, b, :].rearrange("p (h d) -> p h d", h=NH),
                                     AX_X, ALU.add).then_inc(o_ss, 1)
                    dve.wait_ge(o_std, NB * l + b + 1)
                    step.then(v_.reciprocal(rsum[:, 6 * b:6 * b + 6], ss[:, 6 * b:6 * b + 6]))
                    step.then(tt(o3, o3, rsum[:, 6 * b:6 * b + 6].unsqueeze(2).to_broadcast([P, NH, HD]), ALU.mult))
                    tt(o[:, b, :], o[:, b, :], zt[:, b, :], ALU.mult).then_inc(og_ready, 1)
                mixed(1)
                norm(2 * l, (0, 1, 2, 5), lambda q: dve.wait_ge(res_psum, 4 * l + q + 1))
                if l == 0:
                    for q in range(4):
                        dve.wait_ge(xs_hi, q + 1)
                        tt(xs_x[1][:, 2 * q:2 * q + 2, :], ps[:, (4, 3, 6, 7)[q], :].rearrange("p (k t) -> p k t", k=2),
                           xs_x[0][:, 2 * q:2 * q + 2, :].bitcast(F32), ALU.subtract).then_inc(xs_lo, 1)
                    channel_mixer(None, False)
                    norm(1, (0, 1, 2, 3), lambda q: dve.wait_ge(down_part, q + 1) if q < 3 else
                         dve.wait_ge(piece_used, NP))
            for q in range(2, 4):
                dve.wait_ge(xt_psum, 16 + q + 1)
                v_.tensor_copy(xT[:, 2 * q:2 * q + 2, P:T],
                               ps[:, (4, 3, 6, 7)[q], :].rearrange("p (k t) -> p k t", k=2)[:, :, P:T])\
                    .then_inc(xt_dve, 1)
            for b in range(NB):
                dve.wait_ge(xs_hi, 4 + b + 1)
                tt(xs[1][:, b * D:(b + 1) * D], x[:, b, :], xs[0][:, b * D:(b + 1) * D].bitcast(F32),
                   ALU.subtract).then_inc(xs_lo, 1)
            def r8(a, n=16):
                return rt[:, a:a + n].rearrange("p (b e) -> p b e", b=2)

            lg, t8, oh1, oh2, sel_, l2 = (r8(16 * k) for k in range(6))
            m1, m2, ex, g1, g2 = (rt[:, 96 + 2 * k:98 + 2 * k] for k in (3, 4, 2, 5, 6))
            dif = rt[:, 98:100]
            rev = cst[:, C_REV:C_REV + NE].unsqueeze(1).to_broadcast([P, 2, NE])

            def b8(a):
                return a.unsqueeze(2).to_broadcast([P, 2, NE])

            dve.wait_ge(lg_psum, 1)
            step.then(v_.tensor_copy(lg, ps[:, 0, 0:16].rearrange("p (b e) -> p b e", b=2)))

            def first_max(src, m, one_hot):
                step.then(v_.tensor_reduce(m, src, AX_X, ALU.max))
                step.then(tt(t8, src, b8(m), ALU.is_equal))
                step.then(tt(t8, t8, rev, ALU.mult))
                step.then(v_.tensor_reduce(g1, t8, AX_X, ALU.max))
                step.then(tt(one_hot, rev, b8(g1), ALU.is_equal))

            first_max(lg, m1, oh1)
            step.then(stt(l2, oh1, NEG, lg, ALU.mult, ALU.add))
            first_max(l2, m2, oh2)
            tt(dif, m2, m1, ALU.subtract).then_inc(gate_exp_in, 1)
            tt(sel_, oh1, oh2, ALU.add).then_inc(sel_ready, 1)
            dve.wait_ge(gate_exp, 1)
            step.then(ts(g1, ex, 1.0, None, ALU.add))
            step.then(v_.reciprocal(g1, g1))
            step.then(tt(g2, ex, g1, ALU.mult))
            step(tt(oh1, oh1, b8(g1), ALU.mult))
            step.then(tt(oh2, oh2, b8(g2), ALU.mult))
            for e0 in (0, NE):
                step(tt(comb[:, :, e0:e0 + NE], oh1, oh2, ALU.add))
            step(v_.memset(comb[:, :, 16:17], 0.0))
            step(v_.memset(pos[:, :, 16:17], -1.0))
            dve.wait_ge(sel_ready, 1)
            dve.wait_ge(pos_psum, 1)
            step.then(stt(t8, ps[:, 1, 0:16].rearrange("p (b e) -> p b e", b=2), 1000.0, sel_, ALU.add, ALU.mult))
            step(ts(pos[:, :, 0:NE], t8, -1000.0, None, ALU.add))
            step(ts(pos[:, :, NE:2 * NE], t8, -1000.0 - P, None, ALU.add))
            step.then(v_.tensor_reduce(m1[:, 0:1], ps[:, 1, 16:24], AX_X, ALU.max))
            v_.tensor_copy(count_i[:, 0:1], m1[:, 0:1]).then_inc(route_ready, 1)
            dve.wait_ge(route_ready, 1)
            pick_tokens(0)
            gathered(None)
            dve.wait_ge(sc_added, 1)
            dve.wait_ge(lo_ready, NP + PARTS)
            with dve.Fori(0, NE - 1) as i:
                channel_mixer(i, True)
            channel_mixer(NE - 1, False)
            most = dve.value_load(count_i[0:1, 0:1], min_val=0, max_val=T)
            with dve.If(most > P):
                for r in range(PARTS):
                    low_part(NE, r)
                with dve.Fori(NE, 2 * NE - 1) as i:
                    channel_mixer(i, True)
                channel_mixer(2 * NE - 1, False)
            norm(3, None, None)

        @block.tensor
        def _(pe):
            mm, tr = nc.tensor.matmul, nc.tensor.transpose

            def chunk(l, c):
                pe.wait_ge(slot_loaded[c % SLOTS], 16 * (2 * l + c // SLOTS + 1))

            def transpose_x(n, banks, blocks=range(NB)):
                for b in blocks:
                    if n:
                        pe.wait_ge(x_ready, NB * (n - 1) + b + 1)
                    for k in range(KT):
                        c0 = (k % 2) * T + b * P
                        ins = tr(ps[:, banks[k // 2], c0:c0 + P], x[:, b, k * P:(k + 1) * P], ident)
                        if (b or n == 3) and k % 2:
                            ins.then_inc(xt_psum, 1)
                if n in (0, 2):
                    pe.wait_ge(xt_act, n + 2)
                    pe.wait_ge(xt_dve, n + 2)

            def features(bank, col, w, c0, last=None):
                for k in range(KT):
                    ins = mm(ps[:, bank, col:col + T], w[:, k, c0:c0 + P], xT[:, k, :], start=(k == 0),
                             stop=(k == KT - 1))
                return ins

            def tokens(bank, n, w, c0, b):
                for k in range(KT):
                    ins = mm(ps[:, bank, 0:n], xT[:, k, b * P:(b + 1) * P], w[:, k, c0:c0 + n], start=(k == 0),
                             stop=(k == KT - 1))
                return ins

            PRODUCTS = ((0, hi), (1, hi), (0, lo))

            def gather(i, part):
                if part == 0:
                    pe.wait_ge(pick_ready, at(i, 2, 2))
                    if i is not None:
                        pe.wait_ge(sc_added, i * 4 + 1)
                elif i is not None:
                    pe.wait_ge(xg_hi, at(i, 1, 1))
                bank = 6 if i is None and part else 2
                for k in range(KT):
                    for b in range(NB):
                        ins = mm(ps[:, bank + k // 4, (k % 4) * P:(k % 4 + 1) * P],
                                 xs[part][:, b * D + k * P:b * D + (k + 1) * P], pick[:, b, :],
                                 start=(b == 0), stop=(b == NB - 1))
                ins.then_inc(xg_psum, 1)

            def channel_mixer(i):
                nb = blocks_of(i)
                hT = hT_d if i is None else hT_e
                tok = xs if i is None else xg
                nt = T if i is None else P
                for r in range(NP):
                    w, j, p = SEQ[r]
                    pe.wait_ge(lo_ready, at(i, NP, r + 1))
                    if (w, p) == ("G", 0):
                        if j == 0:
                            if i is None:
                                pe.wait_ge(xs_lo, 4)
                            else:
                                pe.wait_ge(xg_hi, i + 1)
                                pe.wait_ge(xg_lo, i + 1)
                        elif i is None and j > 1:
                            pe.wait_ge(ht_lo, j)
                        if j or i is not None:
                            pe.wait_ge(gate_silu, at(i, FC, j))
                    if (w, p) == ("U", 0) and (j or i is not None):
                        pe.wait_ge(h_ready, at(i, FC, j))
                    if (w, p) == ("D", 0):
                        pe.wait_ge(ht_lo, at(i, FC, j + 1))
                    if w != "D":
                        bank = 4 if w == "G" else 4 + nb
                        for b in range(nb):
                            for k in range(4):
                                kk = 4 * p + k
                                for n, (a, part) in enumerate(PRODUCTS):
                                    ins = mm(ps[:, bank + b, :], tok[a][:, kk * nt + b * P:kk * nt + (b + 1) * P],
                                             tiles_of(part[r % PARTS], r)[:, k, :], start=(kk == 0 and n == 0),
                                             stop=(kk == KT - 1 and n == 2))
                    else:
                        for b in range(nb):
                            for c in range(2):
                                for q in range(2):
                                    h0 = 512 * b + P * (2 * p + q)
                                    for n, (a, part) in enumerate(PRODUCTS):
                                        ins = mm(ps[:, 2 * b + c, :], hT[j % 2][a][:, h0:h0 + P],
                                                 tiles_of(part[r % PARTS], r)[:, q, 512 * c:512 * (c + 1)],
                                                 start=(j == 0 and p == 0 and q == 0 and n == 0),
                                                 stop=(j == FC - 1 and p == 1 and q == 1 and n == 2))
                                if j == FC - 1 and p == 1 and (b, c) != (nb - 1, 1):
                                    ins.then_inc(down_part, 1)
                    ins.then_inc(piece_used, 1)
                    if r in AFTER_H:
                        j = AFTER_H.index(r)
                        pe.wait_ge(h_ready, at(i, FC, j + 1))
                        if i is not None:
                            if j == 0:
                                pe.wait_ge(sc_added, i * 4 + 1)
                            pe.wait_ge(ht_lo, at(i, FC, j))
                        for b in range(nb):
                            for q in range(4):
                                ins = tr(ps[:, h_bank(i, j) + b, q * P:(q + 1) * P],
                                         hh[:, 512 * b + q * P:512 * b + (q + 1) * P], ident)
                        ins.then_inc(ht_psum, 1)
                    if i is None:
                        continue
                    if r == AT["G", 1, 1]:
                        pe.wait_ge(sc_added, i * 4 + 1)
                        for b in range(NB):
                            ins = tr(ps[:, 7, b * P:(b + 1) * P], pick[:, b, :].bitcast(F32), ident)
                        ins.then_inc(pickt_psum, 1)
                    if r == AT["G", FC - 1, 1]:
                        gather(i, 0)
                    if r == AT["D", FC - 2, 1]:
                        gather(i, 1)
                if i is None:
                    return
                pe.wait_ge(pickt_evac, i + 1)
                pe.wait_ge(xg_lo, i + 2)
                pe.wait_ge(ht_lo, at(i, FC, FC))
                for k, bank in enumerate((2, 3, 7, 6)):
                    c, b = divmod(k, 2)
                    pe.wait_ge(ye_lo, i * 2 + (c + 1))
                    for part in range(2):
                        ins = mm(ps[:, bank, :], pickT[:, b * P:(b + 1) * P], ye[part][:, 512 * c:512 * (c + 1)],
                                 start=(part == 0), stop=(part == 1))
                    ins.then_inc(sc_out, 1)

            pe.wait_ge(ident_loaded, 16)
            pe.wait_ge(x_loaded, 32)
            for l in range(L):
                transpose_x(2 * l, (0, 1, 6, 7))
                w = [slot_wide(c % SLOTS, WIN[c][1]) for c in range(len(WIN))]
                chunk(l, 0)
                features(4, 0, w[0], 0)
                features(4, T, w[0], P).then_inc(proj_psum, 1)
                features(5, 0, w[0], 2 * P)
                features(5, T, w[0], 3 * P).then_inc(proj_psum, 1)
                chunk(l, 1)
                features(2, 0, w[1], 0)
                features(2, T, w[1], P).then_inc(proj_psum, 1)
                features(3, 0, w[1], 2 * P)
                features(3, T, w[1], 3 * P).then_inc(proj_psum, 1)

                def s5_in(t):
                    re, im = ((6, 0), (6, 2))[t]
                    for r, bank in ((0, re), (1, im)):
                        for jj in range(4):
                            ins = mm(ps[:, bank + jj // 2, (jj % 2) * T:(jj % 2 + 1) * T], b_pad[:, 4 * t + jj, r, :],
                                     uT[:, t, :], start=True, stop=True)
                    ins.then_inc(bu_psum, 1)

                pe.wait_ge(b_loaded, 16 * (l + 1))
                pe.wait_ge(proj_evac, 13 * l + 1)
                s5_in(0)
                chunk(l, 2)
                pe.wait_ge(proj_evac, 13 * l + 2)
                tokens(4, 384, w[2], 0, 0).then_inc(proj_psum, 1)
                tokens(5, 384, w[2], 0, 1).then_inc(proj_psum, 1)
                chunk(l, 3)
                pe.wait_ge(bu_used, 2 * l + 1)
                features(6, 0, w[3], 0)
                features(6, T, w[3], P).then_inc(proj_psum, 1)
                features(7, 0, w[3], 2 * P)
                features(7, T, w[3], 3 * P).then_inc(proj_psum, 1)
                pe.wait_ge(proj_evac, 13 * l + 6)
                for h in range(NH):
                    bank = (2, 3, 0, 1, 4, 5)[h]
                    j, rows = h // 2, slice(64 * (h % 2), 64 * (h % 2) + 64)
                    mm(ps[:, bank, 0:P], qkm[rows, j, 0:P], qkm[rows, 3 + j, 0:P], start=True, stop=True)
                    mm(ps[:, bank, P:3 * P], qkm[rows, j, P:T], qkm[rows, 3 + j, :], start=True, stop=True)\
                        .then_inc(sc_psum, 1)
                pe.wait_ge(proj_evac, 13 * l + 8)
                pe.wait_ge(sc_evac, NH * l + 2)
                s5_in(1)
                chunk(l, 4)
                pe.wait_ge(sc_evac, NH * l + 4)
                features(0, 0, w[4], 0)
                features(0, T, w[4], P).then_inc(proj_psum, 1)
                features(1, 0, w[4], 2 * P)
                features(1, T, w[4], 3 * P).then_inc(proj_psum, 1)
                chunk(l, 5)
                pe.wait_ge(sc_evac, NH * (l + 1))
                pe.wait_ge(bu_used, 2 * l + 2)
                features(4, 0, w[5], 0).then_inc(proj_psum, 1)
                tokens(5, ZAB, w[5], P, 0).then_inc(proj_psum, 1)
                tokens(2, ZAB, w[5], P, 1).then_inc(proj_psum, 1)
                pe.wait_ge(c_ready, l + 1)
                pe.wait_ge(turned, l + 1)
                pe.wait_ge(states_ready, l + 1)
                for f in range(2):
                    for k in range(8):
                        j, r = 4 * f + k // 2, k % 2
                        ins = mm(ps[:, 3, f * T:(f + 1) * T], c_pad[:, j, r, :], states[r][:, j, :],
                                 start=(k == 0), stop=(k == 7))
                ins.then_inc(y_psum, 1)
                pe.wait_ge(sc_norm, 2 * (l + 1))
                pe.wait_ge(proj_evac, 13 * l + 9)
                for h in range(NH):
                    if h >= 2:
                        pe.wait_ge(pt_evac, NH * l + h - 1)
                    for q in range(3):
                        ins = tr(ps[:, (7, 0)[h % 2], q * P:(q + 1) * P], sc[:, h, q * P:(q + 1) * P], ident)
                    ins.then_inc(pt_psum, 1)
                pe.wait_ge(sq_done, l + 1)
                pe.wait_ge(proj_evac, 13 * (l + 1))
                pe.wait_ge(y_sum, l + 1)
                for q, bank in enumerate((2, 3, 6)):
                    mm(ps[:, bank, :], C("same"), sq[:, 2 * q:2 * q + 2, :], start=True, stop=True)\
                        .then_inc(nrm_psum, 1)
                pe.wait_ge(pt_evac, NH * (l + 1))
                pe.wait_ge(glu_loaded, 16 * (l + 1))
                pe.wait_ge(y_gelu, l + 1)
                for f in range(2):
                    for k in range(2):
                        ins = mm(ps[:, 7, f * T:(f + 1) * T], gw[:, k, f * P:(f + 1) * P], ys[:, k, :],
                                 start=(k == 0), stop=(k == 1))
                ins.then_inc(glu_psum, 1)
                pe.wait_ge(proj_evac, 13 * l + 11)
                for h in range(NH):
                    j, rows = h // 2, slice(64 * (h % 2), 64 * (h % 2) + 64)
                    bank, c0 = ((1, 0), (1, T), (4, 0))[j]
                    vc = slice(h * HD, (h + 1) * HD)
                    mm(ps[rows, bank, c0:c0 + P], mv[:, 0, vc], pT[:, h, 0:P], start=True, stop=True)
                    mm(ps[rows, bank, c0 + P:c0 + T], mv[:, 0, vc], pT[:, h, P:2 * P], start=True, stop=False)
                    ins = mm(ps[rows, bank, c0 + P:c0 + T], mv[:, 1, vc], pT[:, h, 2 * P:3 * P], start=False,
                             stop=True)
                ins.then_inc(pv_psum, 1)
                pe.wait_ge(g_ready, l + 1)
                pe.wait_ge(proj_evac, 13 * (l + 1))
                for q, name in enumerate(("cum", "same", "ch0", "ch1")):
                    ins = mm(ps[:, 5, 12 * q:12 * q + 12], C(name), g_i, start=True, stop=True)
                ins.then_inc(gs_psum, 1)
                pe.wait_ge(tg_ready, l + 1)
                pe.wait_ge(glu_sig, 2 * (l + 1))
                pe.wait_ge(pv_evac, l + 1)
                for q, bank in enumerate((7, 0, 1)):
                    mm(ps[:, bank, :], C("ones"), tg[:, 4 * q:4 * q + 4, :], start=True, stop=True)\
                        .then_inc(gb_psum, 1)
                pe.wait_ge(qk_ready, l + 1)
                pe.wait_ge(silu_done, 3 * (l + 1))
                pe.wait_ge(gs_evac, l + 1)
                pe.wait_ge(nrm_ln, 3 * (l + 1))
                for n in range(12):
                    wh, b, j = n // 6, (n // 3) % 2, n % 3
                    ins = tr(ps[:, (4, 5, 2)[n // 4], (n % 4) * P:(n % 4 + 1) * P],
                             qkv[:, 3 + 3 * wh + j, b * P:(b + 1) * P], ident)
                    if n % 4 == 3:
                        ins.then_inc(kv_psum, 1)
                pe.wait_ge(gb_evac, 3 * (l + 1))
                for i in range(12):
                    if i == 10:
                        pe.wait_ge(kv_evac, 3 * l + 1)
                    r, j, b = i // 6, i % 6 // 2, i % 2
                    rows = slice(64 * r, 64 * r + 64)
                    ins = mm(ps[:, (3, 6, 7, 0, 1, 4)[i // 2], b * T:(b + 1) * T].rearrange("p (w c) -> p w c", w=2),
                             qkv[rows, 3 + j, b * P:(b + 1) * P], qkv[rows, j:j + 4:3, b * P:(b + 1) * P],
                             start=True, stop=True)
                    if b:
                        ins.then_inc(kk_psum, 1)
                for g in range(3):
                    pe.wait_ge(m0_ready, 6 * l + 2 * g + 2)
                    pe.wait_ge(la_ready, 6 * l + (4, 5, 6)[g])
                    for i in range(4):
                        ins = tr(ps[:, (0, 1, 3)[g], i * P:(i + 1) * P], M[0][:, 4 * g + i, :], ident)
                    ins.then_inc(t_psum, 1)
                pe.wait_ge(u_ready, 3 * (l + 1))
                pe.wait_ge(kv_evac, 3 * (l + 1))
                for v in range(5):
                    pe.wait_ge(m_ready, 5 * l + v + 1)
                    for g in range(3):
                        n = 3 * v + g
                        if v == 0:
                            pe.wait_ge(t_ready, 3 * l + g + 1)
                        else:
                            pe.wait_ge(xy_used, 15 * l + n - 2)
                        if n >= 2:
                            pe.wait_ge(a_evac, 15 * l + n - 1)
                        for i in range(4 * g, 4 * g + 4):
                            ins = mm(ps[:, (2, 5)[n % 2], (i % 4) * P:(i % 4 + 1) * P], M[(v + 1) % 2][:, i, :],
                                     Tm[:, i, :], start=True, stop=True)
                        ins.then_inc(a_psum, 1)
                    for g in range(3):
                        n = 3 * v + g
                        pe.wait_ge(a_evac, 15 * l + n + 1)
                        for i in range(4 * g, 4 * g + 4):
                            c0 = (i % 4) * P
                            if v < 4:
                                mm(ps[:, (0, 1, 3)[g], c0:c0 + P], U[:, i, :], A[:, i, :], start=True, stop=True)
                            ins = mm(ps[:, (4, 6, 7)[g], c0:c0 + P], A[:, i, :], U[:, i, :], start=True, stop=True)
                        ins.then_inc(xy_psum, 1)
                pe.wait_ge(xy_used, 15 * (l + 1))
                pe.wait_ge(a_evac, 15 * (l + 1))
                pe.wait_ge(s_zero, l + 1)
                for j in range(3):
                    for b in range(NB):
                        for r in range(2):
                            i = 6 * r + 2 * j + b
                            ins = mm(ps[64 * r:64 * r + 64, j // 2, (j % 2) * T + b * P:(j % 2) * T + (b + 1) * P],
                                     kg[:, b, (2 * j + r) * HD:(2 * j + r + 1) * HD], U[:, i, :],
                                     start=True, stop=True)
                ins.then_inc(w_psum, 2)
                for b in range(NB):
                    for h in range(NH):
                        i = 6 * (h % 2) + 2 * (h // 2) + b
                        ins = mm(ps[:, (2, 5)[b], h * HD:(h + 1) * HD], U[:, i, :],
                                 kv[:, 1, b, h * HD:(h + 1) * HD], start=True, stop=True)
                    ins.then_inc(up_psum_, 1)
                pe.wait_ge(w_evac, 2 * (l + 1))
                wo = [slot_tall((6 + c) % SLOTS) for c in range(2)]

                def project(k, bank_at, first, final):
                    b, c = divmod(bank_at, 2)
                    return mm(ps[:, (0, 1, 2, 5)[bank_at], :], xT[:, k, b * P:(b + 1) * P],
                              wo[k // 4][:, k % 4, 512 * c:512 * (c + 1)], start=first, stop=final)

                for n in range(NC):
                    b, c = divmod(n, 2)
                    rows = slice(64 * c, 64 * c + 64)
                    toks = slice(n * CH, (n + 1) * CH)
                    if n:
                        pe.wait_ge(s_ready, 2 * ((NC - 1) * l + n))
                    for j in range(3):
                        ins = mm(ps[rows, 3, j * P:(j + 1) * P], wT[:, j, toks], S[:, j, :], start=True, stop=True)
                    ins.then_inc(ws_psum, 1)
                    if n:
                        pe.wait_ge(qs_used, NC * l + n)
                    for j in range(3):
                        ins = mm(ps[rows, 4, j * P:(j + 1) * P], qkv[:, j, toks], S[:, j, :], start=True, stop=True)
                    ins.then_inc(qs_psum, 1)
                    pe.wait_ge(vp_ready, NC * l + n + 1)
                    for j in range(3 if n < NC - 1 else 0):
                        ins = mm(ps[:, 6, j * P:(j + 1) * P], kd[rows, b, j * P:(j + 1) * P],
                                 vp[rows, b, j * P:(j + 1) * P], start=True, stop=True)
                        if j == 2:
                            ins.then_inc(su_psum, 1)
                    if c:
                        if b:
                            pe.wait_ge(o_ready, NB * l + 1)
                        for h in range(NH):
                            i = 6 * (h % 2) + 2 * (h // 2) + b
                            ins = mm(ps[:, 7, h * HD:(h + 1) * HD], LA[:, i, 0, :], vp[:, b, h * HD:(h + 1) * HD],
                                     start=True, stop=True)
                        ins.then_inc(av_psum, 1)
                    if n == 0:
                        chunk(l, 6)
                        chunk(l, 7)
                        pe.wait_ge(up_evac, NB * (l + 1))
                        pe.wait_ge(mix_ready, 3 * l + 1)
                    for k in ((0, 1), (2,), (3,), (4,))[n]:
                        for q in range(4):
                            ins = project(k, q, k == 0, False)
                        if k == 3:
                            ins.then_inc(wo_used, 1)
                for b in range(NB):
                    pe.wait_ge(og_ready, NB * l + b + 1)
                    for j in range(3):
                        ins = tr(ps[:, 3 + b, j * P:(j + 1) * P], o[:, b, j * P:(j + 1) * P], ident)
                    ins.then_inc(ot_psum, 1)
                    pe.wait_ge(mix_ready, 3 * l + 2 + b)
                    for c in range(2):
                        for k in range(5, 8):
                            ins = project(k, 2 * b + c, False, k == 7)
                        ins.then_inc(res_psum, 1)
                if l == 0:
                    transpose_x(1, (4, 3, 6, 7))
                    channel_mixer(None)

            rw = par[:, PO["router"]:PO["router"] + KT * NE].rearrange("p (k e) -> p k e", k=KT)
            for b in range(NB):
                transpose_x(3, (4, 3, 6, 7), (b,))
                pe.wait_ge(xt_act, (8, 10)[b])
                if b:
                    pe.wait_ge(xt_dve, 6)
                for k in range(KT):
                    ins = mm(ps[:, 0, NE * b:NE * (b + 1)], xT[:, k, b * P:(b + 1) * P], rw[:, k, :],
                             start=(k == 0), stop=(k == KT - 1))
            ins.then_inc(lg_psum, 1)
            pe.wait_ge(sel_ready, 1)
            sel_ = rt[:, 64:80]
            mm(ps[:, 1, 0:8], C("before"), sel_[:, 0:8], start=True, stop=True)
            mm(ps[:, 1, 8:16], C("ones"), sel_[:, 0:8], start=True, stop=False)
            mm(ps[:, 1, 8:16], C("before"), sel_[:, 8:16], start=False, stop=True)
            mm(ps[:, 1, 16:24], C("ones"), sel_[:, 0:8], start=True, stop=False)
            mm(ps[:, 1, 16:24], C("ones"), sel_[:, 8:16], start=False, stop=True).then_inc(pos_psum, 1)

            pe.wait_ge(xs_lo, 4 + NB)
            gather(None, 0)
            gather(None, 1)
            with pe.Fori(0, NE) as i:
                channel_mixer(i)
            pe.wait_ge(route_ready, 1)
            most = pe.value_load(count_i[0:1, 0:1], min_val=0, max_val=T)
            with pe.If(most > P):
                with pe.Fori(NE, 2 * NE) as i:
                    channel_mixer(i)


def tiles(a):
    return np.moveaxis(a.reshape(*a.shape[:-1], a.shape[-1] // P, P), -1, 0)


def kernel(x, w_in, w_out, s5_lam_re, s5_lam_im, s5_log_dt, s5_b_re, s5_b_im, s5_c_re, s5_c_im, s5_d, s5_glu_w,
           s5_glu_b, gdn_conv_w, gdn_a_log, gdn_dt_bias, gdn_norm_w, ln1_g, ln1_b, ln2_g, ln2_b, ffn_w_gate,
           ffn_w_up, ffn_w_down, moe_router, moe_w_gate, moe_w_up, moe_w_down):
    import concourse.bacc as bacc
    from concourse.bass_utils import run_bass_kernel_spmd

    f32 = np.float32
    arr = {k: np.asarray(v) for k, v in dict(
        x_in=x, w_in=w_in, w_out=w_out, wg=ffn_w_gate, wu=ffn_w_up, wd=ffn_w_down, mg=moe_w_gate, mu=moe_w_up,
        md=moe_w_down).items()}
    G, N, Q = 16, 64, 16
    by_state = lambda a: np.asarray(a).reshape(L, ST, P).transpose(2, 0, 1).reshape(P, L * ST)
    c_lay = np.zeros((P, L, ST, 2, 16), f32)
    b_lay = np.zeros((L, P, ST, 2, P), f32)
    for r, (bb, cc) in enumerate(((np.asarray(s5_b_re), np.asarray(s5_c_re)), (np.asarray(s5_b_im), np.asarray(s5_c_im)))):
        for g in range(G):
            j, half = divmod(g, 2)
            c_lay[64 * half:64 * half + 64, :, j, r, :] = cc[:, g].transpose(2, 0, 1)
            f0 = 16 * (g % 8)
            b_lay[:, f0:f0 + 16, j, r, 64 * half:64 * half + 64] = bb[:, g].transpose(0, 2, 1)
    rows = lambda a: np.broadcast_to(np.asarray(a).reshape(1, -1), (P, np.asarray(a).size))
    par = np.zeros((P, PW), f32)
    for name, v in (("lre", by_state(s5_lam_re)), ("lim", by_state(s5_lam_im)),
                    ("ldt", by_state(np.broadcast_to(np.asarray(s5_log_dt)[:, :, None], (L, G, N)))),
                    ("d", tiles(np.asarray(s5_d).reshape(L, S5W)).reshape(P, -1)),
                    ("gb", tiles(np.asarray(s5_glu_b)).reshape(P, -1)),
                    ("conv", tiles(np.asarray(gdn_conv_w)).transpose(0, 1, 3, 2).reshape(P, -1)),
                    ("alog", rows(gdn_a_log)), ("dtb", rows(gdn_dt_bias)), ("nw", rows(gdn_norm_w)),
                    ("c", c_lay.reshape(P, -1)),
                    ("router", np.asarray(moe_router)[0].reshape(KT, P, NE).transpose(1, 0, 2).reshape(P, -1))):
        par[:, PO[name]:PO[name] + v.shape[1]] = v
    arr["consts"] = constant_table()
    arr["params"] = par
    arr["s5_b"] = b_lay.reshape(L, P, ST * 2 * P)
    arr["glu_w"] = np.asarray(s5_glu_w).reshape(L, 2, P, S5W).transpose(0, 2, 1, 3).reshape(L, P, 512)
    arr["ln"] = np.stack([np.stack([np.asarray(g)[l], np.asarray(b)[l]]) for l in range(L)
                          for g, b in ((ln1_g, ln1_b), (ln2_g, ln2_b))])
    nc = bacc.Bacc("TRN2", target_bir_lowering=False, num_devices=1)
    order = ("x_in", "w_in", "w_out", "consts", "params", "s5_b", "glu_w", "ln", "wg", "wu", "wd", "mg", "mu", "md")
    sent, args = {}, []
    for name in order:
        a = np.ascontiguousarray(arr[name])
        sent[f"in_{name}"] = a
        args.append(nc.dram_tensor(f"in_{name}", a.shape, mybir.dt.from_np(a.dtype), kind="ExternalInput").ap())
    out = nc.dram_tensor("out_0", (1, T, D), F32, kind="ExternalOutput").ap()
    build(nc, *args, out)
    r = run_bass_kernel_spmd(nc, [sent], core_ids=[0])
    return r.results[0]["out_0"]
```
